# Optimizing a Trainium2 kernel written in Bass

```python
import math
import jax, jax.numpy as jnp
from jax import lax
import numpy as np

D_MODEL = 1024
BATCH = 1
SEQ = 1024
DEPTH = 1

CHUNK = 64

CONV_HEAD_DIM = 64
CONV_HEADS = 12
D_CONV = CONV_HEADS * CONV_HEAD_DIM
CONV_WIDTH = 3
SSM_GROUP_CH = 16
SSM_GROUPS = 16
D_SSM = SSM_GROUPS * SSM_GROUP_CH
SSM_STATE = 64
D_IN = 3 * D_CONV + D_SSM
DT_MIN = 0.001
DT_MAX = 0.1

N_EXPERTS = 64
TOP_K = 6
N_EXPERT_GROUPS = 8
TOPK_GROUPS = 4
EXPERTS_PER_GROUP = N_EXPERTS // N_EXPERT_GROUPS
D_EXPERT = 256
D_SHARED = 256
ROUTED_SCALE = 2.5
EXPERT_BLOCK = 256

RMS_EPS = 1e-6

kernel_name = 'hybrid_conv_s5_moe_adaln_block'

def rms_norm(x, g):
    xf = x.astype(jnp.float32)
    y = xf * lax.rsqrt(jnp.mean(xf * xf, axis=-1, keepdims=True) + RMS_EPS)
    return (y * g.astype(jnp.float32)).astype(x.dtype)

def modulate(h, shift, scale):
    return h * (1.0 + scale[:, None, :]) + shift[:, None, :]

def short_conv_mixer(b_gate, c_gate, v, conv_w, conv_b):
    z = c_gate * v
    z = lax.conv_general_dilated(
        z, conv_w[:, None, :].astype(z.dtype), window_strides=(1,),
        padding=[(CONV_WIDTH - 1, 0)], dimension_numbers=('NWC', 'WIO', 'NWC'),
        feature_group_count=z.shape[-1])
    z = z + conv_b.astype(z.dtype)
    return b_gate * z

def _complex_scan_combine(e1, e2):
    a1r, a1i, b1r, b1i = e1
    a2r, a2i, b2r, b2i = e2
    ar = a1r * a2r - a1i * a2i
    ai = a1r * a2i + a1i * a2r
    br = a2r * b1r - a2i * b1i + b2r
    bi = a2r * b1i + a2i * b1r + b2i
    return (ar, ai, br, bi)

def s5_mixer(u, lam_re, lam_im, log_dt, b_re, b_im, c_re, c_im, d_skip, w_glu, b_glu):
    bsz, seq, _ = u.shape
    uf = u.astype(jnp.float32).reshape(bsz, seq, SSM_GROUPS, SSM_GROUP_CH)
    lr = lam_re.astype(jnp.float32)
    li = lam_im.astype(jnp.float32)
    dt = jnp.exp(log_dt.astype(jnp.float32))[:, None]
    mag = jnp.exp(lr * dt)
    ang = li * dt
    ab_re = mag * jnp.cos(ang)
    ab_im = mag * jnp.sin(ang)
    den = lr * lr + li * li
    nr = ab_re - 1.0
    ni = ab_im
    q_re = (nr * lr + ni * li) / den
    q_im = (ni * lr - nr * li) / den
    br = b_re.astype(jnp.float32)
    bi = b_im.astype(jnp.float32)
    bb_re = q_re[..., None] * br - q_im[..., None] * bi
    bb_im = q_re[..., None] * bi + q_im[..., None] * br
    bu_re = jnp.einsum('bsgh,gph->bsgp', uf, bb_re)
    bu_im = jnp.einsum('bsgh,gph->bsgp', uf, bb_im)
    a_re = jnp.broadcast_to(ab_re, bu_re.shape)
    a_im = jnp.broadcast_to(ab_im, bu_im.shape)
    _, _, xs_re, xs_im = lax.associative_scan(
        _complex_scan_combine, (a_re, a_im, bu_re, bu_im), axis=1)
    y = (jnp.einsum('bsgp,ghp->bsgh', xs_re, c_re.astype(jnp.float32))
         - jnp.einsum('bsgp,ghp->bsgh', xs_im, c_im.astype(jnp.float32)))
    y = y + d_skip.astype(jnp.float32).reshape(SSM_GROUPS, SSM_GROUP_CH) * uf
    y = y.reshape(bsz, seq, D_SSM)
    y = jax.nn.gelu(y)
    y = y * jax.nn.sigmoid(y @ w_glu.astype(jnp.float32) + b_glu.astype(jnp.float32))
    return y.astype(u.dtype)

def swiglu(h, w1, w3, w2):
    return (jax.nn.silu(h @ w1) * (h @ w3)) @ w2

def routed_experts(h, w_router, router_bias, w1, w3, w2):
    n_tok, d = h.shape
    scores = jax.nn.sigmoid(h.astype(jnp.float32) @ w_router.astype(jnp.float32))
    biased = scores + router_bias.astype(jnp.float32)
    grp = biased.reshape(n_tok, N_EXPERT_GROUPS, EXPERTS_PER_GROUP)
    grp_score = lax.top_k(grp, 2)[0].sum(-1)
    _, grp_idx = lax.top_k(grp_score, TOPK_GROUPS)
    grp_sel = jnp.any(grp_idx[..., None] == jnp.arange(N_EXPERT_GROUPS), axis=1)
    expert_mask = jnp.repeat(grp_sel, EXPERTS_PER_GROUP, axis=-1)
    masked = jnp.where(expert_mask, biased, -jnp.inf)
    _, e_idx = lax.top_k(masked, TOP_K)
    w_sel = jnp.take_along_axis(scores, e_idx, axis=-1)
    w_sel = w_sel / jnp.sum(w_sel, axis=-1, keepdims=True) * ROUTED_SCALE

    n_assign = n_tok * TOP_K
    m = EXPERT_BLOCK
    n_blocks = -(-(n_assign + N_EXPERTS * (m - 1)) // m)
    n_rows = n_blocks * m
    e_flat = e_idx.reshape(n_assign)
    tok_flat = jnp.arange(n_assign, dtype=jnp.int32) // TOP_K
    w_flat = w_sel.reshape(n_assign)
    order = jnp.argsort(e_flat)
    e_sorted = e_flat[order]
    counts = jnp.bincount(e_flat, length=N_EXPERTS)
    padded = (counts + m - 1) // m * m
    start = jnp.cumsum(counts) - counts
    pend = jnp.cumsum(padded)
    pstart = pend - padded
    rank = jnp.arange(n_assign, dtype=jnp.int32) - start[e_sorted]
    dest = pstart[e_sorted] + rank
    tok_buf = jnp.zeros((n_rows,), jnp.int32).at[dest].set(tok_flat[order])
    w_buf = jnp.zeros((n_rows,), jnp.float32).at[dest].set(w_flat[order])
    block_e = jnp.minimum(
        jnp.searchsorted(pend, jnp.arange(n_blocks) * m, side='right'), N_EXPERTS - 1)

    def expert_block(args):
        tok, wt, e = args
        xb = h[tok]
        yb = swiglu(xb, w1[e], w3[e], w2[e])
        return yb * wt[:, None].astype(yb.dtype)

    ys = lax.map(expert_block, (tok_buf.reshape(n_blocks, m),
                                w_buf.reshape(n_blocks, m), block_e))
    return jnp.zeros_like(h).at[tok_buf].add(ys.reshape(n_rows, d).astype(h.dtype))

def setup_inputs(seed: int = 0) -> dict:
    key = jax.random.key(seed)
    ks = jax.random.split(key, 32)
    f32 = jnp.float32
    nrm = lambda k, shape, s: jax.random.normal(k, shape, f32) * s
    d = D_MODEL
    n_idx = jnp.arange(SSM_STATE, dtype=f32)
    return {
        'x': nrm(ks[0], (BATCH, SEQ, d), 1.0),
        'c': nrm(ks[1], (BATCH, d), 1.0),
        'w_ada': nrm(ks[2], (d, 6 * d), 0.02),
        'b_ada': nrm(ks[3], (6 * d,), 0.01),
        'g_mix': 1.0 + nrm(ks[4], (d,), 0.01),
        'w_in': nrm(ks[5], (d, D_IN), d ** -0.5),
        'conv_w': nrm(ks[6], (CONV_WIDTH, D_CONV), CONV_WIDTH ** -0.5),
        'conv_b': nrm(ks[7], (D_CONV,), 0.01),
        'g_conv': 1.0 + nrm(ks[8], (D_CONV,), 0.01),
        'lam_re': -0.5 + nrm(ks[9], (SSM_GROUPS, SSM_STATE), 0.01),
        'lam_im': math.pi * n_idx[None, :] + nrm(ks[10], (SSM_GROUPS, SSM_STATE), 0.01),
        'log_dt': jax.random.uniform(ks[11], (SSM_GROUPS,), f32,
                                     math.log(DT_MIN), math.log(DT_MAX)),
        'b_re': nrm(ks[12], (SSM_GROUPS, SSM_STATE, SSM_GROUP_CH), (2 * SSM_GROUP_CH) ** -0.5),
        'b_im': nrm(ks[13], (SSM_GROUPS, SSM_STATE, SSM_GROUP_CH), (2 * SSM_GROUP_CH) ** -0.5),
        'c_re': nrm(ks[14], (SSM_GROUPS, SSM_GROUP_CH, SSM_STATE), SSM_STATE ** -0.5),
        'c_im': nrm(ks[15], (SSM_GROUPS, SSM_GROUP_CH, SSM_STATE), SSM_STATE ** -0.5),
        'd_skip': nrm(ks[16], (D_SSM,), 1.0),
        'w_glu': nrm(ks[17], (D_SSM, D_SSM), D_SSM ** -0.5),
        'b_glu': nrm(ks[18], (D_SSM,), 0.01),
        'g_ssm': 1.0 + nrm(ks[19], (D_SSM,), 0.01),
        'w_out': nrm(ks[20], (d, d), d ** -0.5),
        'g_ffn': 1.0 + nrm(ks[21], (d,), 0.01),
        'w_router': nrm(ks[22], (d, N_EXPERTS), d ** -0.5),
        'router_bias': nrm(ks[23], (N_EXPERTS,), 0.01),
        'w1': nrm(ks[24], (N_EXPERTS, d, D_EXPERT), d ** -0.5),
        'w3': nrm(ks[25], (N_EXPERTS, d, D_EXPERT), d ** -0.5),
        'w2': nrm(ks[26], (N_EXPERTS, D_EXPERT, d), D_EXPERT ** -0.5),
        'ws1': nrm(ks[27], (d, D_SHARED), d ** -0.5),
        'ws3': nrm(ks[28], (d, D_SHARED), d ** -0.5),
        'ws2': nrm(ks[29], (D_SHARED, d), D_SHARED ** -0.5),
        'g_final': 1.0 + nrm(ks[30], (d,), 0.01),
    }

def reference(x, c, w_ada, b_ada, g_mix, w_in, conv_w, conv_b, g_conv,
              lam_re, lam_im, log_dt, b_re, b_im, c_re, c_im, d_skip, w_glu, b_glu,
              g_ssm, w_out, g_ffn, w_router, router_bias, w1, w3, w2,
              ws1, ws3, ws2, g_final):
    bsz, seq, d = x.shape
    mod = jax.nn.silu(c) @ w_ada + b_ada
    shift1, scale1, gate1, shift2, scale2, gate2 = jnp.split(mod, 6, axis=-1)
    for _ in range(DEPTH):
        h = modulate(rms_norm(x, g_mix), shift1, scale1)
        proj = h @ w_in
        b_gate, c_gate, v, u = jnp.split(
            proj, [D_CONV, 2 * D_CONV, 3 * D_CONV], axis=-1)
        y_conv = rms_norm(short_conv_mixer(b_gate, c_gate, v, conv_w, conv_b), g_conv)
        y_ssm = rms_norm(s5_mixer(u, lam_re, lam_im, log_dt, b_re, b_im, c_re, c_im,
                                  d_skip, w_glu, b_glu), g_ssm)
        y = jnp.concatenate([y_conv, y_ssm], axis=-1) @ w_out
        x = x + gate1[:, None, :] * y
        h2 = modulate(rms_norm(x, g_ffn), shift2, scale2).reshape(bsz * seq, d)
        ffn = swiglu(h2, ws1, ws3, ws2) + routed_experts(h2, w_router, router_bias, w1, w3, w2)
        x = x + gate2[:, None, :] * ffn.reshape(bsz, seq, d)
    return rms_norm(x, g_final)


_drawn_inputs = setup_inputs


def setup_inputs(seed=0):
    import zlib

    import numpy as np

    out = dict(_drawn_inputs(seed))
    spreads = {}
    factors = {'g_mix': 2.742,
     'conv_b': 23.598,
     'g_conv': 14.136,
     'lam_re': 64.0,
     'b_glu': 8.0,
     'g_ssm': 27.375,
     'g_final': 30.982,
     'g_ffn': 3.736}
    for name, (base, spread) in spreads.items():
        noise = np.random.default_rng([zlib.crc32(name.encode()), seed]).standard_normal(out[name].shape)
        drawn = base * np.exp(spread * noise) if base else spread * noise
        out[name] = __import__('jax').numpy.asarray(drawn.astype(out[name].dtype))
    for name, factor in factors.items():
        out[name] = (out[name] * factor).astype(out[name].dtype)
    return out
```

```python
from contextlib import ExitStack

import concourse.bass as bass
from concourse import mybir

ALU = mybir.AluOpType
ACT = mybir.ActivationFunctionType
AX = mybir.AxisListType
F32 = mybir.dt.float32
BF16 = mybir.dt.bfloat16
I32 = mybir.dt.int32
U32 = mybir.dt.uint32

P = 128
EPS = 1e-6
PI = 3.1415925
TWO_PI_HI, TWO_PI_MID, TWO_PI_LO = 6.28125, 0.0019350051879882812, 3.0199159819516e-07
ROUND = 12582912.0
BIG = 1e30
KIB = 1024


class Steps:

    def __init__(self, eng, sem):
        self.eng, self.sem, self.n = eng, sem, 0

    def run(self, ins):
        self.n += 1
        ins.then_inc(self.sem, 1)

    def settle(self):
        self.eng.wait_ge(self.sem, self.n)

    def __call__(self, ins):
        self.run(ins)
        self.settle()


def layer_kernel(nc, x, c, w_ada, b_ada, g_mix, w_in, conv_w, conv_b, g_conv, lam_re, lam_im, log_dt,
                 b_re, b_im, c_re, c_im, d_skip, w_glu, b_glu, g_ssm, w_out, g_ffn, w_router,
                 router_bias, w1, w3, w2, ws1, ws3, ws2, g_final, out):
    _, SEQ, D = x.shape
    NT = SEQ // P
    KC = D // P
    D_CONV = conv_w.shape[1]
    NM = D_CONV // P
    G, S, H = b_re.shape
    D_SSM = G * H
    D_IN = w_in.shape[1]
    NE, _, FE = w1.shape
    TOP_K, NGRP, TOP_G = 6, 8, 4
    EPG = NE // NGRP
    ROUTED_SCALE = 2.5
    FK = FE // P
    MAX_BLOCKS = (SEQ * TOP_K + NE * (P - 1)) // P + 1
    PAIRS = MAX_BLOCKS // 2
    CAP = SEQ // P
    ROWS = SEQ + P
    PIECE = 384
    NP = 6 * D // PIECE
    NP1 = -(-2 * D // PIECE)
    assert NT == 8 and KC == 8 and D_SSM == 2 * P and S == 64 and FK == 2

    with ExitStack() as ctx:
        names = set()

        def sem(name):
            assert name not in names
            names.add(name)
            return ctx.enter_context(nc.semaphore(name))

        base = (nc.sbuf_base + 63) // 64 * 64

        def at(name, offset, shape, dt=F32):
            return nc.alloc_sbuf_tensor_at(name, shape, dt, offset=base + int(offset))

        RX, RH, RW = 0, 32 * KIB, 64 * KIB
        RS = RW + 73 * KIB
        RC = RS + 66.25 * KIB
        x_tok = at("x_tok", RX, [P, NT, D])
        V = at("V", RX, [P, G, 2 * NT - 1, H])
        Vs = at("Vs", RX + 15 * KIB, [P, G, NT, H])
        U = at("U", RX + 24 * KIB, [P, G, NT, H])
        yc = at("yc", RX, [P, NM, SEQ])
        ys = at("ys", RX + 24 * KIB, [P, 2, SEQ])
        hT = at("hT", RH, [P, KC, SEQ])
        x1 = at("x1", RH, [P, NT, D])
        wada = at("wada", RW, [P, 2, KC, PIECE])
        win = at("win", RW + 24 * KIB, [P, 2, 3, KC, P])
        cs = at("cs", RW + 48 * KIB, [P, 512])
        z = at("z", RW + 50 * KIB, [P, NT + 2, P])
        wu = at("wu", RW + 55 * KIB, [P, KC, D_SSM])
        sq = at("sq", RW + 55 * KIB, [P, SEQ])
        sqsum = at("sqsum", RW + 59 * KIB, [P, SEQ])
        acc = at("acc", RW + 63 * KIB, [P, PIECE])
        row = at("row", RW + 64.5 * KIB, [1, 2, PIECE])
        wglu = at("wglu", RW + 67.5 * KIB, [P, 2, D_SSM])
        dskip = at("dskip", RW + 69.5 * KIB, [P, D_SSM])
        bglu = at("bglu", RW + 70.5 * KIB, [P, D_SSM])
        wout = at("wout", RW, [P, KC, D])
        w13 = [at(f"w13_{b}", RW + 24 * KIB * b, [P, 2, KC, FE]) for b in range(2)]
        w2t = [at(f"w2_{b}", RW + 24 * KIB * b + 16 * KIB, [P, FK, D]) for b in range(2)]
        ws13 = at("ws13", RW + 48 * KIB, [P, 2, KC, FE])
        ws2t = at("ws2t", RW + 64 * KIB, [P, FK, D])
        T = at("T", RS, [P, G, P])
        y = at("y", RS, [P, G, NT, H])
        ST = at("ST", RS + 8 * KIB, [P, G, P])
        STs = at("STs", RS + 16 * KIB, [P, G, P])
        Q = at("Q", RS + 24 * KIB, [P, G, NT, H])
        Qs = at("Qs", RS + 32 * KIB, [P, G, NT, H])
        cosT = at("cosT", RS + 40 * KIB, [P, G, P])
        sinT = at("sinT", RS + 48 * KIB, [P, G, P])
        y2 = at("y2", RS + 40 * KIB, [P, NT, D_SSM])
        glu = at("glu", RS + 48 * KIB, [P, NT, D_SSM])
        UT = at("UT", RS + 56 * KIB, [P, 4, P])
        zin = at("zin", RS + 58 * KIB, [P, 4, P])
        zt = at("zt", RS + 60 * KIB, [P, 4, P])
        R1 = at("R1", RS + 62 * KIB, [P, 4, P + 1])
        R2 = at("R2", RS + 62 * KIB + 2080, [P, 4, P + 1])
        W0 = at("W0", RS + 8 * KIB, [P, 2, G, H])
        C0 = at("C0", RS + 56 * KIB, [P, 2, G, H])
        Cn = at("Cn", RS + 10 * KIB, [P, 2, 2, P])
        tp = at("tp", RS + 58 * KIB, [P, 4, 512])
        par = at("par", RS + 12 * KIB, [G, 24, S])
        pdup = at("pdup", RS + 18 * KIB, [G, 7, P])
        h2T = at("h2T", RS, [P, KC, SEQ])
        h2 = at("h2", RS + 32 * KIB, [P, 2, D])
        gate1 = at("gate1", RS + 40 * KIB, [P, D])
        scale2 = at("scale2", RS + 44 * KIB, [P, D])
        shift2 = at("shift2", RS + 48 * KIB, [P, D])
        junk = at("junk", RS + 52 * KIB, [P, D])
        gffn = at("gffn", RS + 56 * KIB, [P, D])
        wr = at("wr", RS + 60 * KIB, [P, KC, NE])
        sig = at("sig", RS + 32 * KIB, [P, NT, NE])
        bia = at("bia", RS + 34 * KIB, [P, NT, NE])
        eq6 = at("eq6", RS + 36 * KIB, [P, NT, NE, TOP_K])
        cmpg = at("cmpg", RS + 36 * KIB, [P, 2, NT, NGRP, NGRP])
        sel = at("sel", RS + 48 * KIB, [P, NT, NE])
        selb = at("selb", RS + 50 * KIB, [P, NT, NE], BF16)
        rs1 = at("rs1", RS + 51 * KIB, [P, NT, NE])
        m8 = at("m8", RS + 53 * KIB, [P, NT, NGRP, 8])
        xg = [at(f"xg{b}", RS + (32 + 4 * b) * KIB, [P, D]) for b in range(2)]
        xgT = [at(f"xgT{b}", RS + (40 + 4 * b) * KIB, [P, KC, P]) for b in range(2)]
        yo = [at(f"yo{b}", RS + (48 + 4 * b) * KIB, [P, D]) for b in range(2)]
        dest = at("dest", RS + 56 * KIB, [P, NT, NE])
        wparts = at("wparts", RS + 58 * KIB, [P, NT, 3, NE], BF16)
        oneh = [at(f"oneh{b}", RS + (61 + 2 * b) * KIB, [P, NT, P], BF16) for b in range(2)]
        ffn = at("ffn", RS, [P, 4, D])
        res = at("res", RS + 16 * KIB, [P, 4, D])
        gate2 = at("gate2", RS + 32 * KIB, [P, D])
        gfin = at("gfin", RS + 36 * KIB, [P, D])
        hid = [at(f"hid{b}", RX + b * KIB, [P, FE]) for b in range(2)]
        sil = [at(f"sil{b}", RX + (2 + b) * KIB, [P, FE]) for b in range(2)]
        hidT = [at(f"hidT{b}", RX + (4 + b) * KIB, [P, FK, P]) for b in range(2)]
        shy = [at(f"shy{b}", RX + (6 + 4 * b) * KIB, [P, D]) for b in range(2)]
        slotn = at("slotn", RX + 14 * KIB, [P, P])
        blkb = at("blkb", RX + 14.5 * KIB, [P, P])
        tri = at("tri", RX + 15 * KIB, [P, P], BF16)
        onesb = at("onesb", RX + 15.25 * KIB, [P, P], BF16)
        iota_e = at("iota_e", RX + 15.5 * KIB, [P, NE])
        rb = at("rb", RX + 15.75 * KIB, [P, NE])
        lowg = at("lowg", RX + 16 * KIB, [P, NGRP, NGRP])
        rsm = at("rsm", RX + 16.25 * KIB, [P, 16, NE])
        cmp8 = at("cmp8", RX + 20.25 * KIB, [P, NE, CAP])
        blk_row = at("blk_row", RX + 22.25 * KIB, [1, P], I32)
        zrow = at("zrow", RX + 24 * KIB, [P, D])
        pre = at("pre", RX + 28 * KIB, [P, NT, NE])
        off = [RC]

        def small(name, cols, dt=F32, rows=P):
            t = at(name, off[0], [rows] + (cols if isinstance(cols, list) else [cols]), dt)
            n = 1
            for v in (cols if isinstance(cols, list) else [cols]):
                n *= v
            off[0] += (n * (2 if dt == BF16 else 4) + 31) // 32 * 32
            return t

        ident = small("ident", P)
        ones = small("ones", 1)
        eps = small("eps", 1)
        sc = small("sc", KC)
        ccol = small("ccol", KC)
        mcol = small("mcol", [4, KC])
        ss = small("ss", [5, NT])
        rs = small("rs", [5, NT])
        cw = small("cw", [3, NM])
        cb = small("cb", NM)
        gc = small("gc", NM)
        gs = small("gs", 2)
        sp = small("sp", [7, G])
        pw = small("pw", [2, G])
        pwt = small("pwt", [4, G])
        trash = small("trash", 2)
        wv = [small(f"wv{b}", [NT, 6], BF16) for b in range(2)]
        slot_id = [small(f"slot_id{b}", 1, I32) for b in range(2)]
        row_id = [small(f"row_id{b}", 1, I32) for b in range(2)]
        idt = small("idt", 4)
        slot_w = [small(f"slot_w{b}", 1) for b in range(2)]
        nblk = small("nblk", 1, I32)
        eblk = small("eblk", 2)
        eblk_i = small("eblk_i", 1, I32)
        dtc = small("dtc", 4, rows=G)
        top8 = small("top8", [NT, 8])
        topi = small("topi", [NT, 8], U32)
        part = small("part", 1)
        assert base + off[0] <= nc.sbuf_usable_end, (base + off[0], nc.sbuf_usable_end)

        ps = ctx.enter_context(nc.psum_tensor("ps", [P, 8, 512], F32))

        mod_d = nc.dram_tensor("mod_d", [6 * D], F32).ap()
        h2_d = nc.dram_tensor("h2_d", [ROWS, D], F32).ap()
        ffn_d = nc.dram_tensor("ffn_d", [ROWS, D], F32).ap()
        blk_d = nc.dram_tensor("blk_d", [P], I32).ap()

        x_v = x.rearrange("b (c i) d -> (b c) i d", i=NT)
        out_v = out.rearrange("b (c i) d -> (b c) i d", i=NT)
        h2_v = h2_d[0:SEQ, :].rearrange("(c i) d -> c i d", i=NT)
        ffn_v = ffn_d[0:SEQ, :].rearrange("(c i) d -> c i d", i=NT)
        wada_v = w_ada.rearrange("(p k) n -> p k n", k=KC)
        win_v = w_in.rearrange("(p k) n -> p k n", k=KC)
        row_of = lambda v: v.rearrange("(o n) -> o n", o=1)
        bcast = lambda v, n: bass.AP(tensor=v.tensor, offset=v.offset, ap=[[0, n]] + [list(e) for e in v.ap])
        modrow = lambda j: bcast(mod_d[j * D:(j + 1) * D], P)

        s_consts = sem("consts")
        s_small = sem("small_loads")
        s_cvec = sem("c_loaded")
        s_s5in = sem("s5_loads")
        s_x = [sem(f"x_loaded{i}") for i in range(NT)]
        s_ada = [sem(f"w_ada_loaded{b}") for b in range(2)]
        s_wu = sem("w_u_loaded")
        s_win = [sem(f"w_in_loaded{b}") for b in range(2)]
        s_silc = sem("silu_c")
        s_gemv = sem("ada_partials")
        s_adar = sem("ada_reduced")
        s_row = sem("ada_row")
        s_rowst = [sem(f"ada_stored{b}") for b in range(2)]
        s_mcol = sem("mod_columns")
        s_ssx = sem("x_squares")
        s_xn = sem("x_normed")
        s_xt = sem("x_transposed")
        s_xeA = sem("x_evac_act")
        s_xeD = sem("x_evac_dve")
        s_a1 = sem("scale1_ready")
        s_hA = sem("h_modulated_act")
        s_hD = sem("h_modulated_dve")
        s_dt = sem("dt_ready")
        s_lrdt = sem("lr_dt")
        s_mag = sem("mag_ready")
        s_ang = sem("angle_ready")
        s_sin = sem("sines_ready")
        s_pd = sem("s5_params")
        s_cneg = sem("c_negated")
        s_pt = sem("params_transposed")
        s_pe = sem("params_evacuated")
        s_V = sem("V_ready")
        s_C = sem("C_evacuated")
        s_E = sem("rotations_ready")
        s_Q = sem("Q_ready")
        s_Tm = sem("T_products")
        s_Te = sem("T_evacuated")
        s_u = sem("u_projected")
        s_ue = sem("u_evacuated")
        s_cv = sem("conv_products")
        s_ce = sem("conv_gate_evacuated")
        s_z = sem("conv_z")
        s_y = sem("conv_y")
        s_sq = sem("conv_squares")
        s_sqs = sem("conv_square_sums")
        s_yg = sem("conv_scaled")
        s_ut = sem("uT_transposed")
        s_ute = sem("uT_evacuated")
        s_s = sem("chunk_inputs")
        s_r = sem("states_ready")
        s_ym = sem("ssm_products")
        s_ye = sem("ssm_y")
        s_gel = sem("gelu_done")
        s_gt = sem("gelu_transposed")
        s_gte = sem("gelu_T_evacuated")
        s_gm = sem("glu_products")
        s_gb = sem("glu_biased")
        s_gsg = sem("glu_sigmoid")
        s_y2 = sem("glu_gated")
        s_ss2 = sem("ssm_squares")
        s_st = sem("conv_stats")
        s_y3 = sem("ssm_normed")
        s_yt = sem("ssm_transposed")
        s_yte = sem("ssm_T_evacuated")
        s_wout = sem("w_out_loaded")
        s_bc = sem("mod_rows_loaded")
        s_a2 = sem("scale2_ready")
        s_op = sem("out_products")
        s_x1 = sem("x1_ready")
        s_ssr = sem("x1_squares")
        s_h2 = sem("h2_ready")
        s_h2st = [sem(f"h2_stored{b}") for b in range(2)]
        s_h2t = sem("h2_transposed")
        s_h2e = sem("h2_T_evacuated")
        s_wr = sem("router_loaded")
        s_ws = sem("shared_loaded")
        s_lg = sem("logits_done")
        s_sg = sem("scores_done")
        s_m1 = sem("shared_mm1")
        s_sl = sem("shared_silu")
        s_hd = sem("shared_hidden")
        s_ht = sem("shared_hT")
        s_hte = sem("shared_hT_evac")
        s_m2 = sem("shared_mm2")
        s_sy = sem("shared_rows")
        s_syst = [sem(f"shared_stored{b}") for b in range(2)]
        s_zst = sem("spare_rows_stored")
        s_zr = sem("zero_rows")
        s_rc = sem("router_consts")
        s_sel = sem("selection_ready")
        s_rank = sem("ranks_done")
        s_ranke = sem("ranks_evacuated")
        s_cnt = sem("counts_done")
        s_tab = sem("block_table")
        s_tabst = sem("block_table_stored")
        s_blk = sem("block_row_loaded")
        s_route = sem("routing_ready")
        s_w13 = [sem(f"w13_loaded{b}") for b in range(2)]
        s_w2 = [sem(f"w2_loaded{b}") for b in range(2)]
        s_oneh_w = sem("slot_values_ready")
        s_oneh = sem("onehot_ready")
        s_id = sem("slot_terms")
        s_rid = sem("scatter_ids_ready")
        s_rbl = sem("router_bias_loaded")
        s_tick = sem("waits_taken")
        s_prep = sem("slots_found")
        s_slot = sem("slots_ready")
        s_xg = [sem(f"rows_gathered{b}") for b in range(2)]
        s_xgt = sem("rows_transposed")
        s_xgA = sem("rows_evac_act")
        s_xgD = sem("rows_evac_dve")
        s_e1 = sem("expert_mm1")
        s_esl = sem("expert_silu")
        s_eh = sem("expert_hidden")
        s_eht = sem("expert_hT")
        s_ehe = sem("expert_hT_evac")
        s_e2 = sem("expert_mm2")
        s_ey = sem("expert_rows")
        s_sc = [sem(f"rows_scattered{b}") for b in range(2)]
        s_fin = sem("experts_summed")
        s_ffn = [sem(f"ffn_loaded{j}") for j in range(4)]
        s_fbc = sem("final_rows_loaded")
        s_x2 = sem("x2_ready")
        s_ssf = sem("x2_squares")
        s_res = sem("result_ready")
        s_out = [sem(f"result_stored{j}") for j in range(4)]
        s_rms = sem("rows_rms")
        s_cst = sem("conv_stats_out")
        s_rmsy = sem("mixer_rms")
        s_vec, s_gp = sem("vector_steps"), sem("gpsimd_steps")

        
        def pairs(eng, n_blocks, body):
            body(0)
            with eng.Fori(1, PAIRS) as j:
                with eng.If(n_blocks > 2 * j + 1):
                    body(j)

        def reached(eng, s, n):
            if not (isinstance(n, int) and n == 0):
                eng.wait_ge(s, n)

        block = ctx.enter_context(nc.Block())

        @block.sync
        def _(q):
            def ada(n):
                if n >= 2:
                    q.wait_ge(s_gemv, n - 1)
                    q.wait_ge(s_rowst[n % 2], 16 * (n // 2))
                q.dma_start(wada[:, n % 2], wada_v[:, :, n * PIECE:(n + 1) * PIECE]).then_inc(s_ada[n % 2], 16)
                q.dma_start(row[:, n % 2, :], row_of(b_ada[n * PIECE:(n + 1) * PIECE])).then_inc(s_ada[n % 2], 16)

            def w_in_chunk(m):
                if m >= 2:
                    q.wait_ge(s_cv, 6 * (m - 1))
                for j in range(3):
                    q.dma_start(win[:, m % 2, j], win_v[:, :, j * D_CONV + m * P:j * D_CONV + (m + 1) * P])\
                     .then_inc(s_win[m % 2], 16)

            q.dma_start(ccol[:], c.rearrange("b (p k) -> (b p) k", k=KC)).then_inc(s_cvec, 16)
            ada(0)
            ada(1)
            for i in range(NT):
                q.dma_start(x_tok[:, i], x_v[:, i]).then_inc(s_x[i], 16)
            for n in range(2, NP1):
                ada(n)
            q.dma_start(wu[:], win_v[:, :, 3 * D_CONV:D_IN]).then_inc(s_wu, 16)
            w_in_chunk(0)
            w_in_chunk(1)
            for m in range(2, NM):
                for n in range(NP1 + 2 * (m - 2), NP1 + 2 * (m - 1)):
                    ada(n)
                w_in_chunk(m)
            for n in range(NP1 + 2 * (NM - 2), NP):
                ada(n)
            q.wait_ge(s_gemv, NP)
            q.wait_ge(s_cv, 6 * NM)
            q.dma_start(wout[:], w_out.rearrange("(k p) n -> p k n", p=P)).then_inc(s_wout, 16)
            q.wait_ge(s_rowst[0], 16 * (NP // 2))
            q.wait_ge(s_rowst[1], 16 * (NP // 2))
            for i in range(NT):
                q.dma_start(x1[:, i], x_v[:, i]).then_inc(s_x[i], 16)
            q.wait_ge(s_y2, 1)
            q.wait_ge(s_y3, 1)
            q.dma_start(gffn[:], bcast(g_ffn, P)).then_inc(s_bc, 16)
            q.wait_ge(s_yt, 4)
            for t, j in ((gate1, 2), (shift2, 3), (scale2, 4)):
                q.dma_start(t[:], modrow(j)).then_inc(s_bc, 16)
            q.dma_start(wr[:], w_router.rearrange("(p k) n -> p k n", k=KC)).then_inc(s_wr, 16)
            q.wait_ge(s_yg, NM)
            q.wait_ge(s_st, 1)
            q.dma_start(ws13[:, 0], ws1.rearrange("(p k) n -> p k n", k=KC)).then_inc(s_ws, 16)
            q.dma_start(ws13[:, 1], ws3.rearrange("(p k) n -> p k n", k=KC)).then_inc(s_ws, 16)
            q.dma_start(ws2t[:], ws2.rearrange("(p k) n -> p k n", k=FK)).then_inc(s_ws, 16)
            for i in range(NT):
                q.wait_ge(s_h2, i + 1)
                q.dma_start(h2_v[:, i], h2[:, i % 2]).then_inc(s_h2st[i % 2], 16)
            q.wait_ge(s_zr, 1)
            q.dma_start(h2_d[SEQ:ROWS, :], zrow[:]).then_inc(s_zst, 16)
            q.dma_start(ffn_d[SEQ:ROWS, :], zrow[:]).then_inc(s_zst, 16)
            q.wait_ge(s_tab, 1)
            q.dma_start(blk_d.rearrange("(p o) -> p o", o=1), eblk_i[:]).then_inc(s_tabst, 16)
            q.wait_ge(s_tabst, 16)
            q.dma_start(blk_row[:], row_of(blk_d)).then_inc(s_blk, 16)
            q.wait_ge(s_blk, 16)
            q.wait_ge(s_op, NT)

            def expert(i):
                e = q.value_load(blk_row[0:1, bass.ds(i, 1)], min_val=0, max_val=NE - 1)
                return bass.ds(e, 1)

            def pick(w, e):
                return w[e, :, :].rearrange("e a b -> (e a) b")

            def loads13(i, b):
                e = expert(i)
                q.dma_start(w13[b][:, 0], pick(w1, e).rearrange("(p k) n -> p k n", k=KC)).then_inc(s_w13[b], 16)
                q.dma_start(w13[b][:, 1], pick(w3, e).rearrange("(p k) n -> p k n", k=KC)).then_inc(s_w13[b], 16)
                return e

            def loads2(e, b):
                q.dma_start(w2t[b][:], pick(w2, e).rearrange("(p k) n -> p k n", k=FK)).then_inc(s_w2[b], 16)

            e = loads13(0, 0)
            loads2(e, 0)
            n_blocks = q.value_load(nblk[0:1, 0:1], min_val=0, max_val=MAX_BLOCKS)

            def pair(j):
                reached(q, s_e1, 2 * j)
                e = loads13(2 * j + 1, 1)
                reached(q, s_e2, 2 * j)
                loads2(e, 1)
                reached(q, s_e1, 2 * j + 1)
                e = loads13(2 * j + 2, 0)
                reached(q, s_e2, 2 * j + 1)
                loads2(e, 0)

            pairs(q, n_blocks, pair)
            q.wait_ge(s_fin, 1)
            q.dma_start(gfin[:], bcast(g_final, P)).then_inc(s_fbc, 16)
            q.dma_start(gate2[:], modrow(5)).then_inc(s_fbc, 16)
            for i in range(NT):
                if i >= 4:
                    q.wait_ge(s_x2, i - 3)
                q.dma_start(ffn[:, i % 4], ffn_v[:, i]).then_inc(s_ffn[i % 4], 16)
                if i >= 2:
                    q.wait_ge(s_res, i - 1)
                    q.dma_start(out_v[:, i - 2], res[:, (i - 2) % 4]).then_inc(s_out[(i - 2) % 4], 16)
            for i in range(NT - 2, NT):
                q.wait_ge(s_res, i + 1)
                q.dma_start(out_v[:, i], res[:, i % 4]).then_inc(s_out[i % 4], 16)
            for j in range(4):
                q.wait_ge(s_out[j], 16 * (NT // 4))

        @block.scalar
        def _(act):
            a = nc.scalar
            with nc.allow_non_contiguous_dma(reason="parameters, once"):
                act.dma_start(par[:, 0, :], lam_re).then_inc(s_s5in, 16)
                act.dma_start(par[:, 1, :], lam_im).then_inc(s_s5in, 16)
                act.dma_start(dtc[:, 0:1], log_dt.rearrange("(g o) -> g o", o=1)).then_inc(s_s5in, 16)
                for h, (t, u) in enumerate(((b_re, b_im), (b_im, b_re))):
                    act.dma_start(W0[0:S, h], t.rearrange("g p h -> p g h")).then_inc(s_s5in, 16)
                    act.dma_start(W0[S:2 * S, h], u.rearrange("g p h -> p g h")).then_inc(s_s5in, 16)
                for h, (t, u) in enumerate(((c_re, c_im), (c_im, c_re))):
                    for r in range(2):
                        act.dma_start(Cn[:, h, r, 0:S], t[r * 8:r * 8 + 8].rearrange("g h p -> (g h) p"))\
                           .then_inc(s_s5in, 16)
                        act.dma_start(Cn[:, h, r, S:2 * S], u[r * 8:r * 8 + 8].rearrange("g h p -> (g h) p"))\
                           .then_inc(s_s5in, 16)
                act.dma_start(mcol[:, 2, :], g_mix.rearrange("(p k) -> p k", k=KC)).then_inc(s_small, 16)
                for w in range(3):
                    act.dma_start(cw[:, w, :], conv_w[w].rearrange("(m p) -> p m", p=P)).then_inc(s_small, 16)
                act.dma_start(cb[:], conv_b.rearrange("(m p) -> p m", p=P)).then_inc(s_small, 16)
                act.dma_start(gc[:], g_conv.rearrange("(m p) -> p m", p=P)).then_inc(s_small, 16)
                act.dma_start(gs[:], g_ssm.rearrange("(m p) -> p m", p=P)).then_inc(s_small, 16)
                act.dma_start(dskip[:], bcast(d_skip, P)).then_inc(s_small, 16)
                act.dma_start(bglu[:], bcast(b_glu, P)).then_inc(s_small, 16)
                act.dma_start(wglu[:], w_glu.rearrange("(k p) n -> p k n", p=P)).then_inc(s_small, 16)
            def root(j, i, width, done):
                a.activation(rs[:, j, i], ss[:, j, i], ACT.Sqrt, bias=eps[:, 0:1], scale=1.0 / width).then_inc(done, 1)

            act.wait_ge(s_consts, 1)
            act.wait_ge(s_cvec, 16)
            a.activation(sc[:], ccol[:], ACT.Silu).then_inc(s_silc, 1)
            act.wait_ge(s_s5in, 16 * 15)
            a.activation(dtc[:, 1:2], dtc[:, 0:1], ACT.Exp).then_inc(s_dt, 1)
            act.wait_ge(s_lrdt, 1)
            a.activation(par[:, 3, :], par[:, 2, :], ACT.Exp).then_inc(s_mag, 1)
            a.activation(par[:, 4, :], par[:, 2, :], ACT.Exp, scale=float(NT)).then_inc(s_mag, 1)
            act.wait_ge(s_ang, 1)
            a.activation(par[:, 7, :], par[:, 6, :], ACT.Sin).then_inc(s_sin, 1)
            a.activation(par[:, 8, :], par[:, 6, :], ACT.Sin, scale=0.5).then_inc(s_sin, 1)
            for i in range(NT):
                act.wait_ge(s_x[i], 16)
                if i >= 1:
                    act.wait_ge(s_ssx, i)
                a.activation(hT[:, 7, :], x_tok[:, i], ACT.Square, accum_out=ss[:, 0, i:i + 1]).then_inc(s_ssx, 1)
                act.wait_ge(s_ssx, i + 1)
                root(0, slice(i, i + 1), D, s_rms)
            act.wait_ge(s_ssx, NT)
            for n in range(0, 16, 2):
                i, kq = n // 2, n % 2
                act.wait_ge(s_xt, n + 1)
                a.activation(hT[:, 4 * kq:4 * kq + 4, i * P:(i + 1) * P],
                             ps[:, n % 4, :].rearrange("p (k c) -> p k c", k=4), ACT.Copy).then_inc(s_xeA, 1)
            def store_row(n):
                act.wait_ge(s_row, n + 1)
                act.dma_start(row_of(mod_d[n * PIECE:(n + 1) * PIECE]), row[:, n % 2, :]).then_inc(s_rowst[n % 2], 16)

            for n in range(NP1):
                store_row(n)
            act.wait_ge(s_rowst[0], 16 * ((NP1 + 1) // 2))
            act.wait_ge(s_rowst[1], 16 * (NP1 // 2))
            act.dma_start(mcol[:, 0, :], mod_d[0:D].rearrange("(p k) -> p k", k=KC)).then_inc(s_mcol, 16)
            act.dma_start(mcol[:, 1, :], mod_d[D:2 * D].rearrange("(p k) -> p k", k=KC)).then_inc(s_mcol, 16)
            act.wait_ge(s_a1, 1)
            act.wait_ge(s_xeA, 8)
            act.wait_ge(s_xeD, 8)
            for k in range(4):
                a.activation(hT[:, k, :], hT[:, k, :], ACT.Identity, bias=mcol[:, 0, k:k + 1],
                             scale=mcol[:, 3, k:k + 1]).then_inc(s_hA, 1)
            act.wait_ge(s_V, 1)
            for n in range(4):
                act.wait_ge(s_u, n + 1)
                a.activation(U[:, :, 2 * n:2 * n + 2, :].rearrange("c g j h -> c j g h"),
                             ps[:, n, :].rearrange("c (j g h) -> c j g h", j=2, g=G), ACT.Copy).then_inc(s_ue, 1)
            for n in range(12):
                act.wait_ge(s_Tm, n + 1)
                dst = (T, ST, STs)[n // 4]
                a.activation(dst[:, 4 * (n % 4):4 * (n % 4) + 4, :],
                             ps[:, 4 + n % 4, :].rearrange("p (g c) -> p g c", g=4), ACT.Copy).then_inc(s_Te, 1)

            def s5_ut(n):
                act.wait_ge(s_ut, n + 1)
                if n == 0:
                    act.wait_ge(s_Te, 12)
                    act.wait_ge(s_Q, 1)
                a.activation(UT[:], ps[:, 7, :].rearrange("p (g c) -> p g c", g=4), ACT.Copy).then_inc(s_ute, 1)

            def conv_gate(m, half):
                act.wait_ge(s_cv, 6 * m + 2 * half + 1)
                if m or half:
                    act.wait_ge(s_z, 2 * m + half)
                a.activation(cs[:], ps[:, (6 * m + 2 * half) % 4, :], ACT.Copy).then_inc(s_ce, 1)

            for m in range(NM):
                conv_gate(m, 0)
                conv_gate(m, 1)
                if m in (1, 2):
                    s5_ut(2 * m - 1)
                if m == 4:
                    for n in range(4):
                        act.wait_ge(s_gt, n + 1)
                        a.activation(ys[:, :, 2 * n * P:2 * (n + 1) * P].rearrange("p k (i c) -> p i k c", i=2),
                                     ps[:, 4 + n % 2, :].rearrange("p (i k c) -> p i k c", i=2, k=2),
                                     ACT.Copy).then_inc(s_gte, 1)
                if m == 5:
                    for n in range(4):
                        act.wait_ge(s_gb, n + 1)
                        a.activation(glu[:, 2 * n:2 * n + 2, :], glu[:, 2 * n:2 * n + 2, :],
                                     ACT.Sigmoid).then_inc(s_gsg, 1)
                act.wait_ge(s_y, 2 * (m + 1))
                if m:
                    act.wait_ge(s_sqs, m)
                a.activation(sq[:], yc[:, m, :], ACT.Square).then_inc(s_sq, 1)
                act.wait_ge(s_sq, m + 1)
                a.activation(yc[:, m, :], yc[:, m, :], ACT.Copy, scale=gc[:, m:m + 1]).then_inc(s_yg, 1)
                if m in (0, 1):
                    s5_ut(2 * m)
                for n in (NP1 + 2 * m, NP1 + 2 * m + 1):
                    if n < NP:
                        store_row(n)
                if m == 3:
                    act.wait_ge(s_ye, 4)
                    a.activation(y2[:].rearrange("c i (g h) -> c g i h", h=H), y[:], ACT.Gelu_apprx_tanh).then_inc(s_gel, 1)
            act.wait_ge(s_y2, 1)
            for i in range(NT):
                a.activation(glu[:, i, :], y2[:, i, :], ACT.Square,
                             accum_out=ss[:, 2, i:i + 1]).then_inc(s_ss2, 1)
            act.wait_ge(s_ss2, NT)
            root(2, slice(0, NT), D_SSM, s_rmsy)
            act.wait_ge(s_cst, 1)
            root(1, slice(0, NT), D_CONV, s_rmsy)
            for n in range(4):
                act.wait_ge(s_yt, n + 1)
                for k in range(2):
                    a.activation(ys[:, k, 2 * n * P:2 * (n + 1) * P].rearrange("p (i c) -> p i c", i=2),
                                 ps[:, 4 + n % 2, :].rearrange("p (i k c) -> p i k c", i=2, k=2)[:, :, k, :],
                                 ACT.Copy, scale=gs[:, k:k + 1]).then_inc(s_yte, 1)

            def h2_evac(i):
                act.wait_ge(s_h2t, i + 1)
                for kq in range(2):
                    a.activation(h2T[:, 4 * kq:4 * kq + 4, i * P:(i + 1) * P],
                                 ps[:, 4 + kq, :].rearrange("p (k c) -> p k c", k=4), ACT.Copy).then_inc(s_h2e, 1)

            for i in range(NT):
                act.wait_ge(s_x1, i + 1)
                if i:
                    act.wait_ge(s_ssr, i)
                a.activation(junk[:], x1[:, i], ACT.Square, accum_out=ss[:, 3, i:i + 1]).then_inc(s_ssr, 1)
                act.wait_ge(s_ssr, i + 1)
                root(3, slice(i, i + 1), D, s_rms)
                if i:
                    h2_evac(i - 1)
            h2_evac(NT - 1)
            act.wait_ge(s_lg, NT)
            act.wait_ge(s_h2st[0], 16 * 4)
            act.wait_ge(s_h2st[1], 16 * 4)
            a.activation(sig[:], ps[:, 3, :].rearrange("c (i e) -> c i e", i=NT), ACT.Sigmoid).then_inc(s_sg, 1)
            for i in range(NT + 1):
                if i < NT:
                    act.wait_ge(s_m1, i + 1)
                    if i >= 2:
                        act.wait_ge(s_hd, i - 1)
                    a.activation(sil[i % 2][:], ps[:, i % 2, 0:FE], ACT.Silu).then_inc(s_sl, 1)
                if i:
                    t = i - 1
                    act.wait_ge(s_m2, t + 1)
                    if t >= 2:
                        act.wait_ge(s_syst[t % 2], 16 * (t // 2))
                    a.activation(shy[t % 2][:].rearrange("c (n f) -> c n f", n=2),
                                 ps[:, 4 + 2 * (t % 2):6 + 2 * (t % 2), :], ACT.Copy).then_inc(s_sy, 1)
                    act.wait_ge(s_sy, t + 1)
                    act.dma_start(ffn_v[:, t], shy[t % 2][:]).then_inc(s_syst[t % 2], 16)

            act.wait_ge(s_xgt, 1)
            a.activation(xgT[0][:, 0:4, :], ps[:, 4, :].rearrange("p (k c) -> p k c", k=4), ACT.Copy)\
             .then_inc(s_xgA, 1)
            n_blocks = act.value_load(nblk[0:1, 0:1], min_val=0, max_val=MAX_BLOCKS)

            def pair(j):
                for i, b in ((2 * j + 1, 1), (2 * j + 2, 0)):
                    reached(act, s_e1, i)
                    a.activation(sil[1 - b][:], ps[:, 1 - b, 0:FE], ACT.Silu).then_inc(s_esl, 1)
                    reached(act, s_xgt, i + 1)
                    a.activation(xgT[b][:, 0:4, :], ps[:, 4, :].rearrange("p (k c) -> p k c", k=4),
                                 ACT.Copy).then_inc(s_xgA, 1)
                    reached(act, s_e2, i)
                    reached(act, s_sc[1 - b], 16 * j)
                    a.activation(yo[1 - b][:].rearrange("c (n f) -> c n f", n=2), ps[:, 6:8, :], ACT.Copy)\
                     .then_inc(s_ey, 1)

            pairs(act, n_blocks, pair)
            last = (n_blocks // 2) * 2
            act.wait_ge(s_e1, last + 1)
            a.activation(sil[0][:], ps[:, 0, 0:FE], ACT.Silu).then_inc(s_esl, 1)
            act.wait_ge(s_e2, last + 1)
            act.wait_ge(s_sc[0], 16 * (n_blocks // 2))
            a.activation(yo[0][:].rearrange("c (n f) -> c n f", n=2), ps[:, 6:8, :], ACT.Copy).then_inc(s_ey, 1)
            for i in range(NT):
                act.wait_ge(s_x2, i + 1)
                if i:
                    act.wait_ge(s_ssf, i)
                a.activation(shy[0][:], x1[:, i], ACT.Square, accum_out=ss[:, 4, i:i + 1]).then_inc(s_ssf, 1)
                act.wait_ge(s_ssf, i + 1)
                root(4, slice(i, i + 1), D, s_rms)

        @block.tensor
        def _(pe):
            t = nc.tensor
            pe.wait_ge(s_consts, 1)
            pe.wait_ge(s_pd, 1)
            for j in range(7):
                mm = t.transpose(ps[:, 7, j * G:(j + 1) * G], pdup[:, j, :], ident[0:G, 0:G])
            mm.then_inc(s_pt, 1)
            pe.wait_ge(s_cneg, 2)
            for h in range(2):
                for r in range(2):
                    mm = t.transpose(ps[:, 6, (2 * h + r) * P:(2 * h + r + 1) * P], Cn[:, h, r, :], ident[:])
            mm.then_inc(s_pt, 1)
            for n in range(16):
                i, kq = n // 2, n % 2
                pe.wait_ge(s_xn, i + 1)
                if n >= 4:
                    pe.wait_ge(s_xeA if n % 2 == 0 else s_xeD, n // 2 - 1)
                for k in range(4):
                    mm = t.transpose(ps[:, n % 4, k * P:(k + 1) * P],
                                     x_tok[:, i].rearrange("c (p k) -> c k p", k=KC)[:, 4 * kq + k, :], ident[:])
                mm.then_inc(s_xt, 1)

            def ada_row(n):
                pe.wait_ge(s_gemv, n + 1)
                if n:
                    pe.wait_ge(s_row, n)
                t.matmul(ps[0:1, 6, 0:PIECE], ones[:, 0:1], acc[:], start=True, stop=True).then_inc(s_adar, 1)

            pe.wait_ge(s_C, 1)
            for n in range(NP1):
                ada_row(n)
            pe.wait_ge(s_hA, 4)
            pe.wait_ge(s_hD, 4)
            pe.wait_ge(s_wu, 16)
            for j in range(NT):
                for k in range(KC):
                    mm = t.matmul(ps[:, j // 2, (j % 2) * D_SSM:(j % 2 + 1) * D_SSM], hT[:, k, j * P:(j + 1) * P],
                                  wu[:, k, :], start=(k == 0), stop=(k == KC - 1))
                if j % 2:
                    mm.then_inc(s_u, 1)
            pe.wait_ge(s_V, 1)
            pe.wait_ge(s_pe, 1)
            pe.wait_ge(s_row, NP1)
            for n in range(12):
                if n >= 4:
                    pe.wait_ge(s_Te, n - 3)
                for gq in range(4):
                    g = 4 * (n % 4) + gq
                    o = ps[:, 4 + n % 4, gq * P:(gq + 1) * P]
                    if n < 4:
                        for i in range(NT):
                            mm = t.matmul(o[:, i * H:(i + 1) * H],
                                          V[:, g, NT - 1 - i:2 * NT - 1 - i, :].rearrange("p m h -> p (m h)"),
                                          C0[:, 0, g, :], start=True, stop=True)
                    else:
                        src = V[:, g, 0:NT, :] if n < 8 else Vs[:, g, :, :]
                        mm = t.transpose(o, src.rearrange("p m h -> p (m h)"), ident[:])
                mm.then_inc(s_Tm, 1)
            pe.wait_ge(s_Te, 12)

            def conv_group(m, n):
                half, j = (n - 4, 0) if n >= 4 else (n // 2, 1 + n % 2)
                if m == 0 and n < 4:
                    pe.wait_ge(s_ue, 4)
                elif n == 0:
                    pe.wait_ge(s_ce, 2 * m)
                elif n == 1:
                    pe.wait_ge(s_z, 2 * m)
                elif n in (2, 3):
                    pe.wait_ge(s_y, 2 * m - 3 + n)
                elif n == 4:
                    pe.wait_ge(s_ce, 2 * m + 1)
                else:
                    pe.wait_ge(s_z, 2 * m + 1)
                for k in range(KC):
                    mm = t.matmul(ps[:, (6 * m + n) % 4, :], win[:, m % 2, j, k, :],
                                  hT[:, k, half * 512:(half + 1) * 512], start=(k == 0), stop=(k == KC - 1))
                mm.then_inc(s_cv, 1)

            def s5_in(n):
                if n:
                    pe.wait_ge(s_ye, n)
                for gq in range(4):
                    mm = t.transpose(ps[:, 7, gq * P:(gq + 1) * P],
                                     U[:, 4 * n + gq].rearrange("c j h -> c (j h)"), ident[:])
                mm.then_inc(s_ut, 1)
                pe.wait_ge(s_ute, n + 1)
                if n:
                    pe.wait_ge(s_r, n)
                for gq in range(4):
                    g = 4 * n + gq
                    t.matmul(ps[:, 4, gq * P:(gq + 1) * P], ST[:, g, :], UT[:, gq, :], start=True, stop=True)
                    mm = t.matmul(ps[:, 5, gq * P:(gq + 1) * P], STs[:, g, :], UT[:, gq, :], start=True, stop=True)
                mm.then_inc(s_s, 1)

            def s5_out(n):
                pe.wait_ge(s_r, n + 1)
                for gq in range(4):
                    g = 4 * n + gq
                    o = ps[:, 7, gq * P:(gq + 1) * P]
                    t.matmul(o, UT[:, gq, :], T[:, g, :], start=True, stop=False)
                    t.matmul(o, R1[:, gq, 0:P], Q[:, g].rearrange("p i h -> p (i h)"), start=False, stop=False)
                    mm = t.matmul(o, R2[:, gq, 0:P], Qs[:, g].rearrange("p i h -> p (i h)"), start=False, stop=True)
                mm.then_inc(s_ym, 1)

            for m in range(NM):
                pe.wait_ge(s_win[m % 2], 48 * (m // 2 + 1))
                for n in range(4):
                    conv_group(m, n)
                if m < 5:
                    ada_row(NP1 + 2 * m)
                if m in (1, 2):
                    s5_out(2 * m - 2)
                    s5_in(2 * m - 1)
                if m == 4:
                    pe.wait_ge(s_gel, 1)
                    for n in range(4):
                        if n >= 2:
                            pe.wait_ge(s_gte, n - 1)
                        for q4 in range(4):
                            i, k = 2 * n + q4 // 2, q4 % 2
                            mm = t.transpose(ps[:, 4 + n % 2, q4 * P:(q4 + 1) * P],
                                             y2[:, i, k * P:(k + 1) * P], ident[:])
                        mm.then_inc(s_gt, 1)
                conv_group(m, 4)
                conv_group(m, 5)
                if m < 5:
                    ada_row(NP1 + 2 * m + 1)
                if m == 0:
                    s5_in(0)
                if m == 1:
                    s5_out(1)
                    s5_in(2)
                if m == 2:
                    s5_out(3)
                if m == 4:
                    pe.wait_ge(s_gte, 4)
                    pe.wait_ge(s_row, NP)
                    for n in range(4):
                        for i in (2 * n, 2 * n + 1):
                            for k in range(2):
                                mm = t.matmul(ps[:, (4, 5, 7, 6)[n], (i % 2) * D_SSM:(i % 2 + 1) * D_SSM],
                                              ys[:, k, i * P:(i + 1) * P], wglu[:, k, :],
                                              start=(k == 0), stop=(k == 1))
                        mm.then_inc(s_gm, 1)
            pe.wait_ge(s_sqs, NM)
            pe.wait_ge(s_gb, 4)
            for i in range(NT):
                mm = t.matmul(ps[:, 6, i:i + 1], sqsum[:, i * P:(i + 1) * P], ones[:, 0:1], start=True, stop=True)
            mm.then_inc(s_st, 1)
            pe.wait_ge(s_y3, 1)
            for n in range(4):
                if n >= 2:
                    pe.wait_ge(s_yte, 2 * (n - 1))
                for q4 in range(4):
                    i, k = 2 * n + q4 // 2, q4 % 2
                    mm = t.transpose(ps[:, 4 + n % 2, q4 * P:(q4 + 1) * P], y2[:, i, k * P:(k + 1) * P], ident[:])
                mm.then_inc(s_yt, 1)
            pe.wait_ge(s_wout, 16)
            pe.wait_ge(s_yg, NM)
            pe.wait_ge(s_yte, 8)

            def h2_transpose(i):
                pe.wait_ge(s_h2, i + 1)
                if i:
                    pe.wait_ge(s_h2e, 2 * i)
                for k in range(KC):
                    mm = t.transpose(ps[:, 4 + k // 4, (k % 4) * P:(k % 4 + 1) * P],
                                     h2[:, i % 2].rearrange("c (p k) -> c k p", k=KC)[:, k, :], ident[:])
                mm.then_inc(s_h2t, 1)

            for i in range(NT):
                if i >= 2:
                    pe.wait_ge(s_x1, i - 1)
                for n in range(2):
                    for k in range(KC):
                        lhs = yc[:, k, i * P:(i + 1) * P] if k < NM else ys[:, k - NM, i * P:(i + 1) * P]
                        mm = t.matmul(ps[:, 2 * (i % 2) + n, :], lhs, wout[:, k, n * 512:(n + 1) * 512],
                                      start=(k == 0), stop=(k == KC - 1))
                mm.then_inc(s_op, 1)
                if i:
                    h2_transpose(i - 1)
            h2_transpose(NT - 1)
            pe.wait_ge(s_wr, 16)
            pe.wait_ge(s_x1, NT)
            pe.wait_ge(s_h2e, 2 * NT)
            for i in range(NT):
                for k in range(KC):
                    mm = t.matmul(ps[:, 3, i * NE:(i + 1) * NE], h2T[:, k, i * P:(i + 1) * P], wr[:, k, :],
                                  start=(k == 0), stop=(k == KC - 1))
                mm.then_inc(s_lg, 1)
            pe.wait_ge(s_ws, 48)
            for i in range(NT + 1):
                if i < NT:
                    if i >= 2:
                        pe.wait_ge(s_hd, i - 1)
                    for k in range(KC):
                        mm = t.matmul(ps[:, i % 2, :], h2T[:, k, i * P:(i + 1) * P], ws13[:, :, k, :],
                                      start=(k == 0), stop=(k == KC - 1))
                    mm.then_inc(s_m1, 1)
                if i:
                    b = (i - 1) % 2
                    pe.wait_ge(s_hd, i)
                    if i >= 2:
                        pe.wait_ge(s_hte, i - 1)
                    for k in range(FK):
                        mm = t.transpose(ps[:, 2, k * P:(k + 1) * P],
                                         hid[b][:].rearrange("c (p k) -> c k p", k=FK)[:, k, :], ident[:])
                    mm.then_inc(s_ht, 1)
                    pe.wait_ge(s_hte, i)
                    if i >= 3:
                        pe.wait_ge(s_sy, i - 2)
                    for n in range(2):
                        for k in range(FK):
                            mm = t.matmul(ps[:, 4 + 2 * b + n, :], hidT[b][:, k, :], ws2t[:, k, n * 512:(n + 1) * 512],
                                          start=(k == 0), stop=(k == FK - 1))
                    mm.then_inc(s_m2, 1)
                if i == 5:
                    pe.wait_ge(s_sel, 1)
                    t.matmul(ps[:, 3, :], tri[:], selb[:].rearrange("c i e -> c (i e)"), start=True, stop=True)\
                     .then_inc(s_rank, 1)
                if i == 6:
                    pe.wait_ge(s_ranke, 1)
                    t.matmul(ps[:, 3, :], onesb[:], selb[:].rearrange("c i e -> c (i e)"), start=True, stop=True)\
                     .then_inc(s_cnt, 1)

            def find_slots(i, b):
                pe.wait_ge(s_oneh_w, i + 1)
                pe.wait_ge(s_oneh, i + 1)
                for k in range(NT):
                    mm = t.matmul(ps[:, 3, 8 * b:8 * b + 6], oneh[b][:, k, :], wv[b][:, k, :],
                                  start=(k == 0), stop=(k == NT - 1))
                mm.then_inc(s_prep, 1)

            def rows_in(b):
                for k in range(KC):
                    mm = t.transpose(ps[:, 4 + k // 4, (k % 4) * P:(k % 4 + 1) * P],
                                     xg[b][:].rearrange("c (p k) -> c k p", k=KC)[:, k, :], ident[:])
                mm.then_inc(s_xgt, 1)

            def product1(b):
                for k in range(KC):
                    mm = t.matmul(ps[:, b, :], xgT[b][:, k, :], w13[b][:, :, k, :],
                                  start=(k == 0), stop=(k == KC - 1))
                mm.then_inc(s_e1, 1)

            def hidden_turn(b):
                for k in range(FK):
                    mm = t.transpose(ps[:, 2, (2 * b + k) * P:(2 * b + k + 1) * P],
                                     hid[b][:].rearrange("c (p k) -> c k p", k=FK)[:, k, :], ident[:])
                mm.then_inc(s_eht, 1)

            def product2(b):
                for n in range(2):
                    for k in range(FK):
                        mm = t.matmul(ps[:, 6 + n, :], hidT[b][:, k, :], w2t[b][:, k, n * 512:(n + 1) * 512],
                                      start=(k == 0), stop=(k == FK - 1))
                mm.then_inc(s_e2, 1)

            pe.wait_ge(s_route, 1)
            find_slots(0, 0)
            pe.wait_ge(s_slot, 1)
            find_slots(1, 1)
            pe.wait_ge(s_sy, NT)
            pe.wait_ge(s_xg[0], 16)
            rows_in(0)
            pe.wait_ge(s_xgA, 1)
            pe.wait_ge(s_xgD, 1)
            pe.wait_ge(s_w13[0], 32)
            product1(0)
            n_blocks = pe.value_load(nblk[0:1, 0:1], min_val=0, max_val=MAX_BLOCKS)

            def pair(j):
                for i, b, mine, prior in ((2 * j + 1, 1, j + 1, j + 1), (2 * j + 2, 0, j + 2, j + 1)):
                    reached(pe, s_xg[b], 16 * mine)
                    reached(pe, s_xgA, i)
                    reached(pe, s_xgD, i)
                    rows_in(b)
                    reached(pe, s_eh, i)
                    reached(pe, s_ehe, i - 1)
                    hidden_turn(1 - b)
                    reached(pe, s_slot, i + 1)
                    find_slots(i + 1, 1 - b)
                    reached(pe, s_ehe, i)
                    reached(pe, s_w2[1 - b], 16 * prior)
                    reached(pe, s_ey, i - 1)
                    product2(1 - b)
                    reached(pe, s_xgA, i + 1)
                    reached(pe, s_xgD, i + 1)
                    reached(pe, s_w13[b], 32 * mine)
                    product1(b)

            pairs(pe, n_blocks, pair)
            last = (n_blocks // 2) * 2
            pe.wait_ge(s_eh, last + 1)
            hidden_turn(0)
            pe.wait_ge(s_ehe, last + 1)
            pe.wait_ge(s_w2[0], 16 * (n_blocks // 2) + 16)
            pe.wait_ge(s_ey, last)
            product2(0)

        @block.vector
        def _(dve):
            v = nc.vector
            step = Steps(dve, s_vec)

            R = lambda j: par[:, j, :]
            tt, ts = v.tensor_tensor, v.tensor_scalar
            dve.wait_ge(s_dt, 1)
            tt(R(2), R(0), dtc[:, 1:2].to_broadcast([G, S]), ALU.mult).then_inc(s_lrdt, 1)
            step(tt(R(5), R(1), dtc[:, 1:2].to_broadcast([G, S]), ALU.mult))
            step(ts(R(6), R(5), 1.0 / (2 * 3.141592653589793), ROUND, ALU.mult, ALU.add))
            step(ts(R(6), R(6), ROUND, None, ALU.subtract))
            step(v.scalar_tensor_tensor(R(5), R(6), -TWO_PI_HI, R(5), ALU.mult, ALU.add))
            step(v.scalar_tensor_tensor(R(5), R(6), -TWO_PI_MID, R(5), ALU.mult, ALU.add))
            step(v.scalar_tensor_tensor(R(5), R(6), -TWO_PI_LO, R(5), ALU.mult, ALU.add))
            ts(R(6), R(5), PI, -PI, ALU.min, ALU.max).then_inc(s_ang, 1)
            dve.wait_ge(s_sin, 2)
            dve.wait_ge(s_mag, 2)
            step(tt(R(9), R(8), R(8), ALU.mult))
            step(ts(R(9), R(9), -2.0, 1.0, ALU.mult, ALU.add))
            step.run(tt(R(10), R(3), R(9), ALU.mult))
            step.run(tt(R(11), R(3), R(7), ALU.mult))
            step.run(tt(R(12), R(0), R(0), ALU.mult))
            step.run(tt(R(13), R(1), R(1), ALU.mult))
            step.settle()
            step.run(tt(R(12), R(12), R(13), ALU.add))
            step.run(ts(R(14), R(10), -1.0, None, ALU.add))
            step.settle()
            step.run(v.reciprocal(R(13), R(12)))
            step.run(tt(R(15), R(14), R(0), ALU.mult))
            step.run(tt(R(16), R(11), R(1), ALU.mult))
            step.run(tt(R(17), R(11), R(0), ALU.mult))
            step.run(tt(R(18), R(14), R(1), ALU.mult))
            step.settle()
            step.run(tt(R(15), R(15), R(16), ALU.add))
            step.run(tt(R(17), R(17), R(18), ALU.subtract))
            step.settle()
            step.run(tt(R(15), R(15), R(13), ALU.mult))
            step.run(tt(R(17), R(17), R(13), ALU.mult))
            cur = (9, 7)
            for n in range(3):
                nxt = (19, 20) if n % 2 == 0 else (21, 22)
                step.run(tt(R(23), R(cur[1]), R(cur[1]), ALU.mult))
                step.run(tt(R(nxt[1]), R(cur[0]), R(cur[1]), ALU.mult))
                step.settle()
                step.run(ts(R(nxt[0]), R(23), -2.0, 1.0, ALU.mult, ALU.add))
                step.run(ts(R(nxt[1]), R(nxt[1]), 2.0, None, ALU.mult))
                step.settle()
                cur = nxt
            for j, r in enumerate((10, 11, 15, 17, cur[0], cur[1], 4)):
                step.run(v.tensor_copy(pdup[:, j, 0:S], R(r)))
                step.run(v.tensor_copy(pdup[:, j, S:2 * S], R(r)))
            step.settle()
            step(v.memset(z[:, 0:2, 0:1], 0.0))
            ts(dtc[:, 2:3], dtc[:, 1:2], 1.0, None, ALU.mult).then_inc(s_pd, 1)
            ts(Cn[:, 0, :, S:2 * S], Cn[:, 0, :, S:2 * S], -1.0, None, ALU.mult).then_inc(s_cneg, 1)
            ts(Cn[:, 1, :, :], Cn[:, 1, :, :], -1.0, None, ALU.mult).then_inc(s_cneg, 1)
            dve.wait_ge(s_pt, 1)
            v.tensor_copy(sp[:].rearrange("p a g -> p (a g)"), ps[:, 7, 0:7 * G]).then_inc(s_pe, 1)
            dve.wait_ge(s_pt, 2)
            v.tensor_copy(C0[:].rearrange("p a g h -> p (a g h)"), ps[:, 6, :]).then_inc(s_C, 1)

            one = lambda i: slice(i, i + 1)
            for i in range(NT):
                dve.wait_ge(s_rms, i + 1)
                step(v.reciprocal(rs[:, 0, one(i)], rs[:, 0, one(i)]))
                ts(x_tok[:, i], x_tok[:, i], rs[:, 0, one(i)], None, ALU.mult).then_inc(s_xn, 1)
            dve.wait_ge(s_ssx, NT)
            for n in range(1, 16, 2):
                i, kq = n // 2, n % 2
                dve.wait_ge(s_xt, n + 1)
                v.tensor_copy(hT[:, 4 * kq:4 * kq + 4, i * P:(i + 1) * P],
                              ps[:, n % 4, :].rearrange("p (k c) -> p k c", k=4)).then_inc(s_xeD, 1)

            def partials(n):
                dve.wait_ge(s_ada[n % 2], 32 * (n // 2 + 1))
                if n:
                    dve.wait_ge(s_adar, n)
                for k in range(KC):
                    w = wada[:, n % 2, k, :]
                    if k == 0:
                        ins = ts(acc[:], w, sc[:, 0:1], None, ALU.mult)
                    else:
                        ins = v.scalar_tensor_tensor(acc[:], w, sc[:, one(k)], acc[:], ALU.mult, ALU.add)
                    if k < KC - 1:
                        step(ins)
                    else:
                        ins.then_inc(s_gemv, 1)

            def add_row(n):
                dve.wait_ge(s_adar, n + 1)
                tt(row[:, n % 2, :], row[:, n % 2, :], ps[0:1, 6, 0:PIECE], ALU.add).then_inc(s_row, 1)

            dve.wait_ge(s_silc, 1)
            for n in range(NP1):
                partials(n)
                add_row(n)
            dve.wait_ge(s_mcol, 32)
            dve.wait_ge(s_small, 16 * 10)
            v.scalar_tensor_tensor(mcol[:, 3, :], mcol[:, 1, :], 1.0, mcol[:, 2, :], ALU.add, ALU.mult)\
             .then_inc(s_a1, 1)
            dve.wait_ge(s_a1, 1)
            dve.wait_ge(s_xeA, 8)
            dve.wait_ge(s_xeD, 8)
            for k in range(4, 8):
                ts(hT[:, k, :], hT[:, k, :], mcol[:, 3, one(k)], mcol[:, 0, one(k)], ALU.mult, ALU.add)\
                 .then_inc(s_hD, 1)

            def conv_z(m, half):
                dve.wait_ge(s_ce, 2 * m + half + 1)
                dve.wait_ge(s_cv, 6 * m + 2 * half + 2)
                tt(z[:, 2 + 4 * half:6 + 4 * half, :].rearrange("p i c -> p (i c)"), cs[:],
                   ps[:, (6 * m + 2 * half + 1) % 4, :], ALU.mult).then_inc(s_z, 1)

            def conv(m):
                dve.wait_ge(s_z, 2 * m + 2)
                step(v.tensor_copy(z[:, 0:2, 1:P], z[:, NT:NT + 2, 0:P - 1]))
                o = yc[:, m, :].rearrange("p (i c) -> p i c", i=NT)
                step(ts(o, z[:, 2:2 + NT, :], cw[:, 2, one(m)], cb[:, one(m)], ALU.mult, ALU.add))
                step(v.scalar_tensor_tensor(o, z[:, 1:1 + NT, :], cw[:, 1, one(m)], o, ALU.mult, ALU.add))
                step(v.scalar_tensor_tensor(o, z[:, 0:NT, :], cw[:, 0, one(m)], o, ALU.mult, ALU.add))
                for half in range(2):
                    dve.wait_ge(s_cv, 6 * m + 5 + half)
                    o = yc[:, m, half * 512:(half + 1) * 512]
                    tt(o, o, ps[:, (6 * m + 4 + half) % 4, :], ALU.mult).then_inc(s_y, 1)

            def s5_states(n):
                g = slice(4 * n, 4 * n + 4)
                S4 = ps[:, 4, :].rearrange("p (g c) -> p g c", g=4)
                Ss4 = ps[:, 5, :].rearrange("p (g c) -> p g c", g=4)
                dve.wait_ge(s_s, n + 1)
                if n == 0:
                    dve.wait_ge(s_E, 1)
                    dve.wait_ge(s_Q, 1)
                    step.run(v.memset(R1[:, :, 0:1], 0.0))
                    step.run(v.memset(R2[:, :, 0:1], 0.0))
                step.run(tt(zin[:], S4, cosT[:, g, :], ALU.mult))
                step.run(tt(zt[:], Ss4, sinT[:, g, :], ALU.mult))
                step.settle()
                step(tt(zin[:], zin[:], zt[:], ALU.subtract))
                for gq in range(4):
                    step.run(v.tensor_tensor_scan(zt[:, gq, :], sp[:, 6, 4 * n + gq:4 * n + gq + 1].to_broadcast([P, P]),
                                                  zin[:, gq, :], 0.0, ALU.mult, ALU.add))
                step.settle()
                if n:
                    dve.wait_ge(s_ym, n)
                step(tt(R1[:, :, 1:P + 1], zt[:], cosT[:, g, :], ALU.mult))
                tt(R2[:, :, 1:P + 1], zt[:], sinT[:, g, :], ALU.mult).then_inc(s_r, 1)

            def s5_y(n):
                g = slice(4 * n, 4 * n + 4)
                dve.wait_ge(s_ym, n + 1)
                d = dskip[:, 64 * n:64 * n + 64].rearrange("c (g h) -> c g h", g=4).unsqueeze(2)
                step(tt(zin[:].rearrange("c g (i h) -> c g i h", h=H), U[:, g],
                        d.to_broadcast([P, 4, NT, H]), ALU.mult))
                tt(y[:, g].rearrange("c g i h -> c (g i h)"), zin[:].rearrange("c g s -> c (g s)"), ps[:, 7, :],
                   ALU.add).then_inc(s_ye, 1)

            for m in range(NM):
                if m < 5:
                    partials(NP1 + 2 * m)
                if m == 0:
                    dve.wait_ge(s_V, 1)
                    dve.wait_ge(s_Te, 12)
                conv_z(m, 0)
                conv_z(m, 1)
                if m < 5:
                    add_row(NP1 + 2 * m)
                    partials(NP1 + 2 * m + 1)
                if m in (1, 2):
                    s5_y(2 * m - 2)
                if m == 5:
                    for n in range(4):
                        dve.wait_ge(s_gm, n + 1)
                        tt(glu[:, 2 * n:2 * n + 2, :], ps[:, (4, 5, 7, 6)[n], :].rearrange("c (i d) -> c i d", i=2),
                           bglu[:].unsqueeze(1).to_broadcast([P, 2, D_SSM]), ALU.add).then_inc(s_gb, 1)
                conv(m)
                if m < 5:
                    add_row(NP1 + 2 * m + 1)
                if m == 0:
                    s5_states(0)
                if m == 1:
                    s5_states(1)
                    s5_y(1)
                    s5_states(2)
                if m == 2:
                    s5_states(3)
                    s5_y(3)
                if m == 5:
                    dve.wait_ge(s_gsg, 4)
                    tt(y2[:], y2[:], glu[:], ALU.mult).then_inc(s_y2, 1)
            dve.wait_ge(s_st, 1)
            v.tensor_copy(ss[:, 1, :], ps[:, 6, 0:NT]).then_inc(s_cst, 1)
            dve.wait_ge(s_rmsy, 2)
            step(v.reciprocal(rs[:, 2, :], rs[:, 2, :]))
            step(tt(rs[:, 4, :], rs[:, 1, :], rs[:, 2, :], ALU.mult))
            step(v.reciprocal(rs[:, 1, :], rs[:, 1, :]))
            tt(y2[:], y2[:], rs[:, 4, :].unsqueeze(2).to_broadcast([P, NT, D_SSM]), ALU.mult).then_inc(s_y3, 1)

            dve.wait_ge(s_bc, 64)
            v.scalar_tensor_tensor(scale2[:], scale2[:], 1.0, gffn[:], ALU.add, ALU.mult).then_inc(s_a2, 1)
            dve.wait_ge(s_a2, 1)
            for i in range(NT):
                dve.wait_ge(s_op, i + 1)
                if i >= 2:
                    dve.wait_ge(s_h2st[i % 2], 16 * (i // 2))
                    dve.wait_ge(s_h2t, i - 1)
                b = h2[:, i % 2]
                step(v.scalar_tensor_tensor(b.rearrange("c (n f) -> c n f", n=2),
                                            ps[:, 2 * (i % 2):2 * (i % 2) + 2, :], rs[:, 1, one(i)],
                                            gate1[:].rearrange("c (n f) -> c n f", n=2), ALU.mult, ALU.mult))
                dve.wait_ge(s_x[i], 32)
                tt(x1[:, i], x1[:, i], b, ALU.add).then_inc(s_x1, 1)
                dve.wait_ge(s_rms, NT + i + 1)
                step(v.reciprocal(rs[:, 3, one(i)], rs[:, 3, one(i)]))
                dve.wait_ge(s_x1, i + 1)
                step(v.scalar_tensor_tensor(b, x1[:, i], rs[:, 3, one(i)], scale2[:], ALU.mult, ALU.mult))
                tt(b, b, shift2[:], ALU.add).then_inc(s_h2, 1)

            bc = lambda ap, shape: ap.to_broadcast(shape)
            GS, CG, GB, WS, TOT, NB, PE_, PS_ = range(8)
            small8 = lambda j: rsm[:, j, :].rearrange("c (i g) -> c i g", i=NT)

            def r_groups():
                dve.wait_ge(s_sg, 1)
                dve.wait_ge(s_rc, 2)
                step(tt(bia[:], sig[:], bc(rb[:].unsqueeze(1), [P, NT, NE]), ALU.add))
                for i in range(NT):
                    for g in range(NGRP):
                        step.run(v.max(m8[:, i, g, :], bia[:, i, g * EPG:(g + 1) * EPG]))
                step.settle()
                step(tt(small8(GS), m8[:, :, :, 0], m8[:, :, :, 1], ALU.add))

            def r_group_choice():
                a_ = bc(small8(GS).unsqueeze(2), [P, NT, NGRP, NGRP])
                b_ = bc(small8(GS).unsqueeze(3), [P, NT, NGRP, NGRP])
                step.run(tt(cmpg[:, 0], a_, b_, ALU.is_gt))
                step.run(tt(cmpg[:, 1], a_, b_, ALU.is_equal))
                step.settle()
                step(tt(cmpg[:, 1], cmpg[:, 1], bc(lowg[:].unsqueeze(1), [P, NT, NGRP, NGRP]), ALU.mult))
                step(tt(cmpg[:, 0], cmpg[:, 0], cmpg[:, 1], ALU.add))
                step(v.tensor_reduce(small8(CG), cmpg[:, 0], AX.X, ALU.add))
                step(ts(small8(CG), small8(CG), float(TOP_G), None, ALU.is_lt))
                step(ts(small8(GB), small8(CG), BIG, -BIG, ALU.mult, ALU.add))
                flat = bia[:].rearrange("c i (g e) -> c i g e", g=NGRP)
                step(tt(flat, flat, bc(small8(CG).unsqueeze(3), [P, NT, NGRP, EPG]), ALU.mult))
                step(tt(flat, flat, bc(small8(GB).unsqueeze(3), [P, NT, NGRP, EPG]), ALU.add))

            def r_top():
                for i in range(NT):
                    step.run(v.max(top8[:, i, :], bia[:, i, :]))
                step.settle()
                for i in range(NT):
                    step.run(v.max_index(topi[:, i, :], top8[:, i, :], bia[:, i, :]))
                step.settle()
                step(v.tensor_copy(top8[:], topi[:]))

            def r_select():
                shape = [P, NT, NE, TOP_K]
                step(tt(eq6[:], bc(iota_e[:].unsqueeze(1).unsqueeze(3), shape),
                        bc(top8[:, :, 0:TOP_K].unsqueeze(2), shape), ALU.is_equal))

            def r_selected():
                step(v.tensor_reduce(sel[:], eq6[:], AX.X, ALU.add))
                v.tensor_copy(selb[:], sel[:]).then_inc(s_sel, 1)

            def r_weights():
                step(tt(rs1[:], sel[:], sig[:], ALU.mult))
                step(v.tensor_reduce(rsm[:, WS, 0:NT], rs1[:], AX.X, ALU.add))
                step(v.reciprocal(rsm[:, WS, NT:2 * NT], rsm[:, WS, 0:NT]))
                step(ts(rsm[:, WS, NT:2 * NT], rsm[:, WS, NT:2 * NT], ROUTED_SCALE, None, ALU.mult))
                step(tt(rs1[:], rs1[:], bc(rsm[:, WS, NT:2 * NT].unsqueeze(2), [P, NT, NE]), ALU.mult))
                step(v.tensor_copy(wparts[:, :, 0, :], rs1[:]))
                step(tt(rs1[:], rs1[:], wparts[:, :, 0, :], ALU.subtract))
                step(v.tensor_copy(wparts[:, :, 1, :], rs1[:]))
                step(tt(rs1[:], rs1[:], wparts[:, :, 1, :], ALU.subtract))
                step(v.tensor_copy(wparts[:, :, 2, :], rs1[:]))

            def r_ranks():
                dve.wait_ge(s_rank, 1)
                v.tensor_copy(dest[:].rearrange("c i e -> c (i e)"), ps[:, 3, :]).then_inc(s_ranke, 1)

            def r_blocks():
                cnt = ps[:, 3, :].rearrange("c (i e) -> c i e", i=NT)
                dve.wait_ge(s_cnt, 1)
                dve.wait_ge(s_ranke, 1)
                step(v.memset(pre[:, 0, :], 0.0))
                for i in range(NT - 1):
                    step(tt(pre[:, i + 1, :], pre[:, i, :], cnt[:, i, :], ALU.add))
                step(tt(rsm[:, TOT, :], pre[:, NT - 1, :], cnt[:, NT - 1, :], ALU.add))
                step.run(tt(dest[:], dest[:], pre[:], ALU.add))
                step(tt(cmp8[:], bc(rsm[:, TOT, :].unsqueeze(2), [P, NE, CAP]),
                        bc(blkb[:, 0:CAP].unsqueeze(1), [P, NE, CAP]), ALU.is_gt))
                step(v.tensor_reduce(rsm[:, NB, :], cmp8[:], AX.X, ALU.add))
                step(v.tensor_tensor_scan(rsm[:, PE_, :], ones[:, 0:1].to_broadcast([P, NE]), rsm[:, NB, :], 0.0,
                                          ALU.mult, ALU.add))
                step(tt(rsm[:, PS_, :], rsm[:, PE_, :], rsm[:, NB, :], ALU.subtract))
                step(ts(rsm[:, PS_, :], rsm[:, PS_, :], float(P), 1.0, ALU.mult, ALU.add))
                step(tt(dest[:], dest[:], bc(rsm[:, PS_, :].unsqueeze(1), [P, NT, NE]), ALU.add))
                step(tt(dest[:], dest[:], sel[:], ALU.mult))
                step(ts(dest[:], dest[:], -1.0, None, ALU.add))
                step(ts(rsm[:, NB, :], rsm[:, PE_, :], part[:, 0:1], None, ALU.is_le))
                step(v.tensor_reduce(eblk[:, 0:1], rsm[:, NB, :], AX.X, ALU.add))
                step(v.tensor_copy(nblk[:], rsm[:, PE_, NE - 1:NE]))
                ts(eblk_i[:], eblk[:, 0:1], float(NE - 1), None, ALU.min).then_inc(s_tab, 1)

            portions = {0: [r_groups], 1: [r_group_choice, r_top], 2: [r_select], 3: [r_selected, r_weights],
                        5: [r_ranks], 6: [r_blocks]}
            for i in range(NT + 1):
                if i < NT:
                    b = i % 2
                    dve.wait_ge(s_sl, i + 1)
                    dve.wait_ge(s_m1, i + 1)
                    if i >= 2:
                        dve.wait_ge(s_ht, i - 1)
                    tt(hid[b][:], sil[b][:], ps[:, b, FE:2 * FE], ALU.mult).then_inc(s_hd, 1)
                if i:
                    b = (i - 1) % 2
                    dve.wait_ge(s_ht, i)
                    if i >= 3:
                        dve.wait_ge(s_m2, i - 2)
                    v.tensor_copy(hidT[b][:].rearrange("p k c -> p (k c)"), ps[:, 2, 0:2 * P]).then_inc(s_hte, 1)
                for portion in portions.get(i, []):
                    portion()

            def onehot(i, b):
                e = dve.value_load(blk_row[0:1, bass.ds(i, 1)], min_val=0, max_val=NE - 1)
                v.tensor_copy(wv[b][:, :, 3:6], wparts[:, :, :, bass.ds(e, 1)].rearrange("c i w e -> c i (w e)"))\
                 .then_inc(s_oneh_w, 1)
                v.scalar_tensor_tensor(oneh[b][:], bc(dest[:, :, bass.ds(e, 1)], [P, NT, P]),
                                       blkb[:, bass.ds(i, 1)], bc(slotn[:].unsqueeze(1), [P, NT, P]),
                                       ALU.subtract, ALU.is_equal).then_inc(s_oneh, 1)

            def slots(i, b):
                pv = ps[:, 3, 8 * b:8 * b + 6]
                dve.wait_ge(s_prep, i + 1)
                v.tensor_reduce(idt[:, 0:1], pv[:, 0:2], AX.X, ALU.add).then_inc(s_id, 1)
                ts(idt[:, 1:2], pv[:, 2:3], trash[:, 1:2], trash[:, 0:1], ALU.mult, ALU.add).then_inc(s_id, 1)
                v.tensor_reduce(slot_w[b][:], pv[:, 3:6], AX.X, ALU.add).then_inc(s_id, 1)
                dve.wait_ge(s_id, 3 * i + 3)
                tt(slot_id[b][:], idt[:, 0:1], idt[:, 1:2], ALU.add).then_inc(s_slot, 1)

            dve.wait_ge(s_blk, 16)
            dve.wait_ge(s_rc, 3)
            onehot(0, 0)
            onehot(1, 1)
            v.memset(eblk[:, 1:2], 0.0).then_inc(s_route, 1)
            slots(0, 0)
            slots(1, 1)
            onehot(2, 0)
            dve.wait_ge(s_xgt, 1)
            v.tensor_copy(xgT[0][:, 4:8, :], ps[:, 5, :].rearrange("p (k c) -> p k c", k=4)).then_inc(s_xgD, 1)
            n_blocks = dve.value_load(nblk[0:1, 0:1], min_val=0, max_val=MAX_BLOCKS)

            def hidden(b):
                v.scalar_tensor_tensor(hid[b][:], sil[b][:], slot_w[b][:, 0:1], ps[:, b, FE:2 * FE],
                                       ALU.mult, ALU.mult).then_inc(s_eh, 1)

            def pair(j):
                for i, b in ((2 * j + 1, 1), (2 * j + 2, 0)):
                    reached(dve, s_esl, i)
                    reached(dve, s_slot, i)
                    hidden(1 - b)
                    reached(dve, s_sc[1 - b], 16 * j)
                    v.tensor_copy(row_id[1 - b][:], slot_id[1 - b][:]).then_inc(s_rid, 1)
                    reached(dve, s_xgt, i + 1)
                    v.tensor_copy(xgT[b][:, 4:8, :], ps[:, 5, :].rearrange("p (k c) -> p k c", k=4))\
                     .then_inc(s_xgD, 1)
                    reached(dve, s_eht, i)
                    v.tensor_copy(hidT[1 - b][:].rearrange("p k c -> p (k c)"),
                                  ps[:, 2, 2 * (1 - b) * P:2 * (2 - b) * P]).then_inc(s_ehe, 1)
                    reached(dve, s_rid, i)
                    slots(i + 1, 1 - b)
                    onehot(i + 2, b)

            pairs(dve, n_blocks, pair)
            dve.wait_ge(s_esl, (n_blocks // 2) * 2 + 1)
            hidden(0)
            dve.wait_ge(s_sc[0], 16 * (n_blocks // 2))
            v.tensor_copy(row_id[0][:], slot_id[0][:]).then_inc(s_rid, 1)
            dve.wait_ge(s_eht, (n_blocks // 2) * 2 + 1)
            v.tensor_copy(hidT[0][:].rearrange("p k c -> p (k c)"), ps[:, 2, 0:2 * P]).then_inc(s_ehe, 1)

            dve.wait_ge(s_fbc, 32)
            for i in range(NT):
                f = ffn[:, i % 4]
                dve.wait_ge(s_ffn[i % 4], 16 * (i // 4 + 1))
                step(tt(f, f, gate2[:], ALU.mult))
                tt(x1[:, i], x1[:, i], f, ALU.add).then_inc(s_x2, 1)
                dve.wait_ge(s_rms, 2 * NT + i + 1)
                step(v.reciprocal(rs[:, 4, one(i)], rs[:, 4, one(i)]))
                if i >= 4:
                    dve.wait_ge(s_out[i % 4], 16 * (i // 4))
                v.scalar_tensor_tensor(res[:, i % 4], x1[:, i], rs[:, 4, one(i)], gfin[:], ALU.mult, ALU.mult)\
                 .then_inc(s_res, 1)

        @block.gpsimd
        def _(gp):
            p = nc.gpsimd
            step = Steps(gp, s_gp)
            tt, ts = p.tensor_tensor, p.tensor_scalar
            step(p.memset(ident[:], 0.0))
            step(p.memset(ones[:], 1.0))
            step(p.memset(eps[:], EPS))
            p.affine_select(out=ident[:], in_=ident[:], compare_op=ALU.not_equal, fill=1.0, base=0,
                            pattern=[[-1, P]], channel_multiplier=1).then_inc(s_consts, 1)
            gp.wait_ge(s_s5in, 16 * 15)
            step(ts(W0[0:S, 1], W0[0:S, 1], -1.0, None, ALU.mult))
            gp.wait_ge(s_pe, 1)
            gp.wait_ge(s_xt, 16)
            tmp = lambda j: tp[:, j, 0:G * H].rearrange("p (g h) -> p g h", g=G)
            wide = lambda ap: ap.unsqueeze(2).to_broadcast([P, G, H])

            def times(re, im, a, a_s, o, o_s):
                step.run(tt(tmp(0), a, wide(re), ALU.mult))
                step.run(tt(tmp(1), a_s, wide(im), ALU.mult))
                step.run(tt(tmp(2), a_s, wide(re), ALU.mult))
                step.run(tt(tmp(3), a, wide(im), ALU.mult))
                step.settle()
                step.run(tt(o, tmp(0), tmp(1), ALU.add))
                step.run(tt(o_s, tmp(2), tmp(3), ALU.subtract))
                step.settle()

            step.run(p.memset(V[:, :, NT:2 * NT - 1, :], 0.0))
            times(sp[:, 2], sp[:, 3], W0[:, 0], W0[:, 1], V[:, :, NT - 1, :], Vs[:, :, NT - 1, :])
            for m in range(NT - 2, -1, -1):
                times(sp[:, 0], sp[:, 1], V[:, :, m + 1, :], Vs[:, :, m + 1, :], V[:, :, m, :], Vs[:, :, m, :])
            step.settle()
            p.memset(pwt[:, 0, 0:1], 0.0).then_inc(s_V, 1)
            gp.wait_ge(s_C, 1)
            times(sp[:, 0], sp[:, 1], C0[:, 0], C0[:, 1], Q[:, :, 0, :], Qs[:, :, 0, :])
            for i in range(1, NT):
                times(sp[:, 0], sp[:, 1], Q[:, :, i - 1, :], Qs[:, :, i - 1, :], Q[:, :, i, :], Qs[:, :, i, :])
            step.run(p.memset(cosT[:, :, 0:1], 1.0))
            step.run(p.memset(sinT[:, :, 0:1], 0.0))
            step.run(p.tensor_copy(pw[:, 0, :], sp[:, 4, :]))
            step.run(p.tensor_copy(pw[:, 1, :], sp[:, 5, :]))
            step.settle()
            n = 1
            half = lambda j, n: tp[:].rearrange("p a b -> p (a b)")[:, 1024 * j:1024 * j + G * n]\
                .rearrange("p (g c) -> p g c", g=G)
            while n < P:
                wr_ = pw[:, 0, :].unsqueeze(2).to_broadcast([P, G, n])
                wi_ = pw[:, 1, :].unsqueeze(2).to_broadcast([P, G, n])
                step.run(tt(half(0, n), cosT[:, :, 0:n], wr_, ALU.mult))
                step(tt(half(1, n), sinT[:, :, 0:n], wi_, ALU.mult))
                step(tt(cosT[:, :, n:2 * n], half(0, n), half(1, n), ALU.subtract))
                step.run(tt(half(0, n), cosT[:, :, 0:n], wi_, ALU.mult))
                step(tt(half(1, n), sinT[:, :, 0:n], wr_, ALU.mult))
                step(tt(sinT[:, :, n:2 * n], half(0, n), half(1, n), ALU.add))
                step.run(tt(pwt[:, 0, :], pw[:, 1, :], pw[:, 1, :], ALU.mult))
                step(tt(pwt[:, 1, :], pw[:, 0, :], pw[:, 1, :], ALU.mult))
                step.run(ts(pw[:, 0, :], pwt[:, 0, :], -2.0, 1.0, ALU.mult, ALU.add))
                step(ts(pw[:, 1, :], pwt[:, 1, :], 2.0, None, ALU.mult))
                n *= 2
            p.memset(pwt[:, 0, 0:1], 0.0).then_inc(s_E, 1)
            p.memset(pwt[:, 1, 0:1], 0.0).then_inc(s_Q, 1)
            for m in range(NM):
                gp.wait_ge(s_sq, m + 1)
                if m == 0:
                    p.tensor_copy(sqsum[:], sq[:]).then_inc(s_sqs, 1)
                else:
                    gp.wait_ge(s_sqs, m)
                    tt(sqsum[:], sqsum[:], sq[:], ALU.add).then_inc(s_sqs, 1)
            gp.wait_ge(s_op, NT)
            p.memset(zrow[:], 0.0).then_inc(s_zr, 1)
            step.run(p.iota(part[:], [[0, 1]], base=0, channel_multiplier=1, allow_small_or_imprecise_dtypes=True))
            step.run(p.iota(trash[:, 0:1], [[0, 1]], base=SEQ, channel_multiplier=1,
                            allow_small_or_imprecise_dtypes=True))
            step.run(p.iota(slotn[:], [[1, P]], base=0, channel_multiplier=0, allow_small_or_imprecise_dtypes=True))
            step.run(p.iota(blkb[:], [[P, P]], base=0, channel_multiplier=0, allow_small_or_imprecise_dtypes=True))
            step.run(p.iota(iota_e[:], [[1, NE]], base=0, channel_multiplier=0, allow_small_or_imprecise_dtypes=True))
            step.run(p.memset(tri[:], 1.0))
            step.run(p.memset(onesb[:], 1.0))
            step.run(p.memset(lowg[:], 1.0))
            for b in range(2):
                step.run(p.iota(wv[b][:, :, 0], [[0, NT]], base=0, channel_multiplier=NT,
                                allow_small_or_imprecise_dtypes=True))
                step.run(p.iota(wv[b][:, :, 1], [[1, NT]], base=0, channel_multiplier=0,
                                allow_small_or_imprecise_dtypes=True))
                step.run(p.memset(wv[b][:, :, 2], 1.0))
            step.settle()
            step.run(ts(trash[:, 1:2], trash[:, 0:1], -1.0, None, ALU.mult))
            step.run(p.affine_select(out=tri[:], in_=tri[:], compare_op=ALU.is_gt, fill=0.0, base=0,
                                     pattern=[[1, P]], channel_multiplier=-1))
            step.run(p.affine_select(out=lowg[:], in_=lowg[:], compare_op=ALU.is_gt, fill=0.0, base=0,
                                     pattern=[[1, NGRP], [-1, NGRP]], channel_multiplier=0))
            gp.dma_start(rb[:], bcast(router_bias, P)).then_inc(s_rbl, 16)
            gp.wait_ge(s_rbl, 16)
            step.settle()
            p.memset(pwt[:, 0, 0:1], 0.0).then_inc(s_rc, 3)

            def gather(b):
                p.indirect_dma_start(out=xg[b][:], out_offset=None, in_=h2_d,
                                     in_offset=bass.IndirectOffsetOnAxis(ap=slot_id[b][:, 0:1], axis=0))\
                 .then_inc(s_xg[b], 16)

            def scatter(b):
                p.indirect_dma_start(out=ffn_d, out_offset=bass.IndirectOffsetOnAxis(ap=row_id[b][:, 0:1], axis=0),
                                     in_=yo[b][:], in_offset=None, compute_op=ALU.add).then_inc(s_sc[b], 16)

            gp.wait_ge(s_h2st[0], 16 * 4)
            gp.wait_ge(s_h2st[1], 16 * 4)
            gp.wait_ge(s_zst, 32)
            gp.wait_ge(s_slot, 1)
            gather(0)
            gp.wait_ge(s_slot, 2)
            gather(1)
            gp.wait_ge(s_syst[0], 16 * 4)
            gp.wait_ge(s_syst[1], 16 * 4)
            n_blocks = gp.value_load(nblk[0:1, 0:1], min_val=0, max_val=MAX_BLOCKS)

            def settled(n):
                reached(gp, s_tick, n)
                tt(pwt[:, 2, 0:1], pwt[:, 3, 0:1], pwt[:, 3, 0:1], ALU.mult).then_inc(s_tick, 1)

            def pair(j):
                for i, b, before in ((2 * j + 1, 1, j), (2 * j + 2, 0, j + 1)):
                    reached(gp, s_slot, i + 2)
                    reached(gp, s_xgt, i)
                    settled(4 * j + 2 * (1 - b))
                    gather(1 - b)
                    reached(gp, s_ey, i)
                    reached(gp, s_rid, i)
                    reached(gp, s_sc[b], 16 * before)
                    settled(4 * j + 2 * (1 - b) + 1)
                    scatter(1 - b)

            step(p.memset(pwt[:, 3, 0:1], 0.0))
            pairs(gp, n_blocks, pair)
            gp.wait_ge(s_ey, (n_blocks // 2) * 2 + 1)
            gp.wait_ge(s_rid, (n_blocks // 2) * 2 + 1)
            gp.wait_ge(s_sc[1], 16 * (n_blocks // 2))
            settled(4 * (n_blocks // 2))
            scatter(0)
            gp.wait_ge(s_sc[0], 16 * (n_blocks // 2) + 16)
            gp.wait_ge(s_xg[1], 16 * (n_blocks // 2) + 16)
            settled(4 * (n_blocks // 2) + 1)
            gp.wait_ge(s_zst, 32)
            p.memset(pwt[:, 0, 0:1], 0.0).then_inc(s_fin, 1)


INPUTS = ["x", "c", "w_ada", "b_ada", "g_mix", "w_in", "conv_w", "conv_b", "g_conv", "lam_re", "lam_im", "log_dt",
          "b_re", "b_im", "c_re", "c_im", "d_skip", "w_glu", "b_glu", "g_ssm", "w_out", "g_ffn", "w_router",
          "router_bias", "w1", "w3", "w2", "ws1", "ws3", "ws2", "g_final"]


def kernel(**inputs):
    import numpy as np
    import concourse.bacc as bacc
    from concourse.bass_utils import run_bass_kernel_spmd

    nc = bacc.Bacc("TRN2", target_bir_lowering=False, num_devices=1)
    arrays, args = {}, []
    for name in INPUTS:
        a = np.ascontiguousarray(inputs[name])
        arrays[f"in_{name}"] = a
        args.append(nc.dram_tensor(f"in_{name}", a.shape, mybir.dt.from_np(a.dtype), kind="ExternalInput").ap())
    out = nc.dram_tensor("out", inputs["x"].shape, F32, kind="ExternalOutput").ap()
    layer_kernel(nc, *args, out)
    r = run_bass_kernel_spmd(nc, [arrays], core_ids=[0])
    return r.results[0]["out"]
```

```python
from contextlib import ExitStack

import concourse.bass as bass
from concourse import mybir

ALU = mybir.AluOpType
ACT = mybir.ActivationFunctionType
AX = mybir.AxisListType
F32 = mybir.dt.float32
BF16 = mybir.dt.bfloat16
F32R = mybir.dt.float32r
I32 = mybir.dt.int32
U32 = mybir.dt.uint32

P = 128
EPS = 1e-6
PI = 3.1415925
TWO_PI_HI, TWO_PI_MID, TWO_PI_LO = 6.28125, 0.0019350051879882812, 3.0199159819516e-07
ROUND = 12582912.0
BIG = 1e30
KIB = 1024


class Steps:

    def __init__(self, eng, sem):
        self.eng, self.sem, self.n = eng, sem, 0

    def run(self, ins):
        self.n += 1
        ins.then_inc(self.sem, 1)

    def settle(self):
        self.eng.wait_ge(self.sem, self.n)

    def __call__(self, ins):
        self.run(ins)
        self.settle()


def layer_kernel(nc, x, c, w_ada, b_ada, g_mix, w_in, conv_w, conv_b, g_conv, lam_re, lam_im, log_dt,
                 b_re, b_im, c_re, c_im, d_skip, w_glu, b_glu, g_ssm, w_out, g_ffn, w_router,
                 router_bias, w1, w3, w2, ws1, ws3, ws2, g_final, out):
    _, SEQ, D = x.shape
    NT = SEQ // P
    KC = D // P
    D_CONV = conv_w.shape[1]
    NM = D_CONV // P
    G, S, H = b_re.shape
    D_SSM = G * H
    D_IN = w_in.shape[1]
    NE, _, FE = w1.shape
    TOP_K, NGRP, TOP_G = 6, 8, 4
    EPG = NE // NGRP
    ROUTED_SCALE = 2.5
    FK = FE // P
    MAX_BLOCKS = (SEQ * TOP_K + NE * P) // P
    PAIRS = MAX_BLOCKS // 2
    RUN = 6
    CAP = SEQ // P
    ROWS = SEQ + P
    PIECE = 256
    NP = 4 * D // PIECE
    RING = 3
    PER_M = 4
    assert (PAIRS - 2) % RUN == 0 and NT == 8 and KC == 8 and D_SSM == 2 * P and S == 64 and FK == 2

    with ExitStack() as ctx:
        names = set()

        def sem(name):
            assert name not in names
            names.add(name)
            return ctx.enter_context(nc.semaphore(name))

        base = (nc.sbuf_base + 63) // 64 * 64

        def at(name, offset, shape, dt=F32):
            return nc.alloc_sbuf_tensor_at(name, shape, dt, offset=base + int(offset))

        RX, RH, RW = 0, 32 * KIB, 64 * KIB
        RS = RW + 73 * KIB
        RC = RS + 66.25 * KIB
        x_tok = at("x_tok", RX, [P, NT, D])
        V = at("V", RX, [P, G, NT, H])
        Vs = at("Vs", RX + 8 * KIB, [P, G, NT, H])
        U = at("U", RX + 24 * KIB, [P, G, NT, H])
        yc = at("yc", RX, [P, NM, SEQ])
        ys = at("ys", RX + 24 * KIB, [P, 2, SEQ])
        hT = at("hT", RH, [P, KC, SEQ])
        x1 = at("x1", RH, [P, NT, D])
        ada0 = [at(f"ada0_{n}", (RW, RS + 24 * KIB)[n], [P, KC, D]) for n in range(2)]
        wada = at("wada", RW, [P, RING, KC, PIECE])
        win = at("win", RW + 24 * KIB, [P, 2, 3, KC, P])
        cs = at("cs", RW + 48 * KIB, [P, 512])
        z = at("z", RW + 50 * KIB, [P, NT + 2, P])
        wu = at("wu", RW + 55 * KIB, [P, KC, D_SSM])
        row0 = at("row0", RW + 32 * KIB, [1, 2, D])
        sq = at("sq", RW + 55 * KIB, [P, SEQ])
        sqsum = at("sqsum", RW + 59 * KIB, [P, SEQ])
        acc = at("acc", RW + 63 * KIB, [P, PIECE])
        row = at("row", RW + 64 * KIB, [1, 4, PIECE])
        ztmp = at("ztmp", RW + 50 * KIB, [P, 4, G * H])
        wglu = at("wglu", RW + 68 * KIB, [P, 2, D_SSM])
        dskip = at("dskip", RW + 70 * KIB, [P, D_SSM])
        bglu = at("bglu", RW + 71 * KIB, [P, D_SSM])
        wout = at("wout", RS + 8 * KIB, [P, KC, D])
        W_LO = 57 * KIB // 4
        W13 = 2 * KC * FE
        w_parts = at("w_parts", RW, [P, W_LO + 3 * W13], F32R)
        w_raw = at("w_raw", RW + 57 * KIB, [P, 3, 2, KC, FE])
        w2t = at("w2t", RW + 32 * KIB, [P, 3, FK, D])
        ws13 = at("ws13", RW + 48 * KIB, [P, 2, KC, FE])
        ws2t = at("ws2t", RW + 64 * KIB, [P, FK, D])
        T = at("T", RS, [P, NT, G, H])
        y = at("y", RX + 24 * KIB, [P, G, NT, H])
        ST = at("ST", RS + 8 * KIB, [P, G, P])
        STs = at("STs", RS + 16 * KIB, [P, G, P])
        Q = at("Q", RS + 24 * KIB, [P, G, NT, H])
        Qs = at("Qs", RS + 32 * KIB, [P, G, NT, H])
        cosT = at("cosT", RS + 40 * KIB, [P, G, P])
        sinT = at("sinT", RS + 48 * KIB, [P, G, P])
        y2 = at("y2", RS + 40 * KIB, [P, NT, D_SSM])
        glu = at("glu", RS + 48 * KIB, [P, NT, D_SSM])
        UT = at("UT", RS + 56 * KIB, [P, 4, P])
        zin = at("zin", RS + 58 * KIB, [P, 4, P])
        zt = at("zt", RS + 60 * KIB, [P, 4, P])
        R1 = at("R1", RS + 62 * KIB, [P, 4, P + 1])
        R2 = at("R2", RS + 62 * KIB + 2080, [P, 4, P + 1])
        W0 = at("W0", RS + 8 * KIB, [P, 2, G, H])
        C0 = at("C0", RS + 56 * KIB, [P, 2, G, H])
        Cn = at("Cn", RS + 10 * KIB, [P, 2, 2, P])
        tp = at("tp", RS + 58 * KIB, [P, 4, 512])
        par = at("par", RS + 12 * KIB, [G, 24, S])
        pdup = at("pdup", RS + 18 * KIB, [G, 7, P])
        h2T = at("h2T", RW, [P, KC, SEQ])
        h2 = at("h2", RW + 32 * KIB, [P, 2, D])
        gate1 = at("gate1", RS + 40 * KIB, [P, D])
        scale2 = at("scale2", RS + 44 * KIB, [P, D])
        shift2 = at("shift2", RS + 48 * KIB, [P, D])
        junk = at("junk", RS + 52 * KIB, [P, D])
        gffn = at("gffn", RS + 56 * KIB, [P, D])
        wr = at("wr", RS + 60 * KIB, [P, KC, NE])
        sig = at("sig", RS + 32 * KIB, [P, NT, NE])
        bia = at("bia", RS + 34 * KIB, [P, NT, NE])
        eq6 = at("eq6", RS + 36 * KIB, [P, NT, NE, TOP_K])
        cmpg = at("cmpg", RS + 36 * KIB, [P, 2, NT, NGRP, NGRP])
        sel = at("sel", RS + 48 * KIB, [P, NT, NE])
        selb = at("selb", RS + 50 * KIB, [P, NT, NE], BF16)
        rs1 = at("rs1", RS + 51 * KIB, [P, NT, NE])
        lgT = at("lgT", RS + 52 * KIB, [NE, SEQ])
        m8 = at("m8", RS + 53 * KIB, [P, NT, NGRP, 8])
        xg = [at(f"xg{b}", RS + (32 + 4 * b) * KIB, [P, D]) for b in range(2)]
        xgh = [at(f"xgh{b}", RS + (40 + 4 * b) * KIB, [P, KC, P], F32R) for b in range(2)]
        xgl = [at(f"xgl{b}", RX + (24 + 4 * b) * KIB, [P, KC, P], F32R) for b in range(2)]
        yo = [at(f"yo{b}", RS + (48 + 4 * b) * KIB, [P, D]) for b in range(2)]
        dest = at("dest", RS + 56 * KIB, [P, NT, NE])
        wparts = at("wparts", RS + 58 * KIB, [P, NT, 3, NE], BF16)
        oneh = [at(f"oneh{b}", RS + (61 + 2 * b) * KIB, [P, NT, P], BF16) for b in range(2)]
        ffn = at("ffn", RW, [P, NT, D])
        res = at("res", RW + 32 * KIB, [P, NT, D])
        gate2 = at("gate2", RX + 16 * KIB, [P, D])
        gfin = at("gfin", RX + 10 * KIB, [P, D])
        hid = [at(f"hid{b}", RX + b * KIB, [P, FE]) for b in range(2)]
        sil = [at(f"sil{b}", RX + (2 + b) * KIB, [P, FE]) for b in range(2)]
        hidT = [at(f"hidT{b}", RX + (4 + b) * KIB, [P, FK, P]) for b in range(2)]
        shy = [at(f"shy{b}", RX + (6 + 4 * b) * KIB, [P, D]) for b in range(2)]
        slotn = at("slotn", RX + 14 * KIB, [P, P])
        blkb = at("blkb", RX + 14.5 * KIB, [P, P])
        tri = at("tri", RX + 15 * KIB, [P, P], BF16)
        onesb = at("onesb", RX + 15.25 * KIB, [P, P], BF16)
        iota_e = at("iota_e", RX + 15.5 * KIB, [P, NE])
        rb = at("rb", RX + 15.75 * KIB, [P, NE])
        lowg = at("lowg", RX + 16 * KIB, [P, NGRP, NGRP])
        rsm = at("rsm", RX + 16.25 * KIB, [P, 16, NE])
        cmp8 = at("cmp8", RX + 20.25 * KIB, [P, NE, CAP])
        blk_row = at("blk_row", RX + 22.25 * KIB, [1, P], I32)
        ends = at("ends", RX + 22.75 * KIB, [1, NE], I32)
        zrow = at("zrow", RX + 24 * KIB, [P, D])
        pre = at("pre", RX + 28 * KIB, [P, NT, NE])
        off = [RC]

        def small(name, cols, dt=F32, rows=P):
            t = at(name, off[0], [rows] + (cols if isinstance(cols, list) else [cols]), dt)
            n = 1
            for v in (cols if isinstance(cols, list) else [cols]):
                n *= v
            off[0] += (n * (2 if dt == BF16 else 4) + 31) // 32 * 32
            return t

        ident = small("ident", P)
        ones = small("ones", 1)
        eps = small("eps", 1)
        sc = small("sc", KC)
        ccol = small("ccol", KC)
        bcol = small("bcol", [2, KC])
        mcol = small("mcol", [4, KC])
        ss = small("ss", [5, NT])
        rs = small("rs", [5, NT])
        cw = small("cw", [3, NM])
        cb = small("cb", NM)
        gc = small("gc", NM)
        gs = small("gs", 2)
        sp = small("sp", [7, G])
        pw = small("pw", [2, G])
        pwt = small("pwt", [4, G])
        trash = small("trash", 2)
        wv = [small(f"wv{b}", [NT, 6], BF16) for b in range(2)]
        slot_id = [small(f"slot_id{b}", 1, I32) for b in range(2)]
        row_id = [small(f"row_id{b}", 1, I32) for b in range(2)]
        idt = small("idt", 4)
        slot_w = [small(f"slot_w{b}", 1) for b in range(2)]
        held_id = [small(f"held_id{b}", 1, I32) for b in range(2)]
        held_w = [small(f"held_w{b}", 1) for b in range(2)]
        nblk = small("nblk", 1, I32)
        eblk = small("eblk", 2)
        eblk_i = small("eblk_i", 1, I32)
        dtc = small("dtc", 4, rows=G)
        top8 = small("top8", [NT, 8])
        topi = small("topi", [NT, 8], U32)
        part = small("part", 1)
        assert base + off[0] <= nc.sbuf_usable_end, (base + off[0], nc.sbuf_usable_end)

        ps = ctx.enter_context(nc.psum_tensor("ps", [P, 8, 512], F32))

        mod_d = nc.dram_tensor("mod_d", [6 * D], F32).ap()
        h2_d = nc.dram_tensor("h2_d", [ROWS, D], F32).ap()
        ffn_d = nc.dram_tensor("ffn_d", [ROWS, D], F32).ap()
        blk_d = nc.dram_tensor("blk_d", [P], I32).ap()

        x_v = x.rearrange("b (c i) d -> (b c) i d", i=NT)
        out_v = out.rearrange("b (c i) d -> (b c) i d", i=NT)
        h2_v = h2_d[0:SEQ, :].rearrange("(c i) d -> c i d", i=NT)
        ffn_v = ffn_d[0:SEQ, :].rearrange("(c i) d -> c i d", i=NT)
        wada_v = w_ada.rearrange("(p k) n -> p k n", k=KC)
        win_v = w_in.rearrange("(p k) n -> p k n", k=KC)
        row_of = lambda v: v.rearrange("(o n) -> o n", o=1)
        bcast = lambda v, n: bass.AP(tensor=v.tensor, offset=v.offset, ap=[[0, n]] + [list(e) for e in v.ap])
        modrow = lambda j: bcast(mod_d[j * D:(j + 1) * D], P)

        s_consts = sem("consts")
        s_small = sem("small_loads")
        s_cvec = sem("c_loaded")
        s_s5in = sem("s5_loads")
        s_x = [sem(f"tile_loaded{i}") for i in range(NT)]
        s_ada0 = [sem(f"w_ada_first{n}") for n in range(4)]
        s_row0 = sem("first_rows")
        s_row0e = sem("first_rows_evacuated")
        s_adac = sem("first_columns")
        s_ada = [sem(f"w_ada_loaded{b}") for b in range(RING)]
        s_brow = sem("b_ada_loaded")
        s_wu = sem("w_u_loaded")
        s_win = [sem(f"w_in_loaded{b}") for b in range(2)]
        s_silc = sem("silu_c")
        s_gemv = sem("ada_partials")
        s_adar = sem("ada_reduced")
        s_row = sem("ada_row")
        s_rowst = sem("ada_stored")
        s_ssx = sem("x_squares")
        s_xn = sem("x_normed")
        s_xt = sem("x_transposed")
        s_xeA = sem("x_evac_act")
        s_xeD = sem("x_evac_dve")
        s_a1 = sem("scale1_ready")
        s_hA = sem("h_modulated_act")
        s_hD = sem("h_modulated_dve")
        s_s5a = sem("s5_by_act")
        s_s5v = sem("s5_by_dve")
        s_cneg = sem("c_negated")
        s_pt = sem("params_transposed")
        s_pe = sem("params_evacuated")
        s_V = sem("V_ready")
        s_C = sem("C_evacuated")
        s_E = sem("rotations_ready")
        s_Q = sem("Q_ready")
        s_T0 = sem("T_cleared")
        s_Tsh = sem("T_shifted")
        s_Tm = sem("T_products")
        s_Te = sem("T_evacuated")
        s_u = sem("u_projected")
        s_ue = sem("u_evacuated")
        s_cv = sem("conv_products")
        s_ce = sem("conv_gate_evacuated")
        s_z = sem("conv_z")
        s_y = sem("conv_y")
        s_sq = sem("conv_squares")
        s_sqs = sem("conv_square_sums")
        s_yg = sem("conv_scaled")
        s_ut = sem("uT_transposed")
        s_ute = sem("uT_evacuated")
        s_s = sem("chunk_inputs")
        s_r = sem("states_ready")
        s_ym = sem("ssm_products")
        s_ye = sem("ssm_y")
        s_gel = sem("gelu_done")
        s_gt = sem("gelu_transposed")
        s_gte = sem("gelu_T_evacuated")
        s_gm = sem("glu_products")
        s_gb = sem("glu_biased")
        s_gsg = sem("glu_sigmoid")
        s_y2 = sem("glu_gated")
        s_ss2 = sem("ssm_squares")
        s_st = sem("conv_stats")
        s_y3 = sem("ssm_normed")
        s_yt = sem("ssm_transposed")
        s_yte = sem("ssm_T_evacuated")
        s_wout = sem("w_out_loaded")
        s_bc = sem("mod_rows_loaded")
        s_op = sem("out_products")
        s_x1 = sem("x1_ready")
        s_ssr = sem("x1_squares")
        s_h2 = sem("h2_ready")
        s_h2st = [sem(f"h2_stored{b}") for b in range(2)]
        s_h2t = sem("h2_transposed")
        s_h2e = sem("h2_T_evacuated")
        s_wr = sem("router_loaded")
        s_ws = sem("shared_loaded")
        s_lg = sem("logits_done")
        s_lge = sem("logits_evacuated")
        s_sg = sem("scores_done")
        s_m1 = sem("shared_mm1")
        s_sl = sem("shared_silu")
        s_hd = sem("shared_hidden")
        s_ht = sem("shared_hT")
        s_hte = sem("shared_hT_evac")
        s_m2 = sem("shared_mm2")
        s_sy = sem("shared_rows")
        s_syst = [sem(f"shared_stored{b}") for b in range(2)]
        s_zst = sem("spare_rows_stored")
        s_zr = sem("zero_rows")
        s_rc = sem("router_consts")
        s_sel = sem("selection_ready")
        s_rank = sem("ranks_done")
        s_ranke = sem("ranks_evacuated")
        s_cnt = sem("counts_done")
        s_tab = sem("block_table")
        s_blk = sem("block_row_loaded")
        s_route = sem("routing_ready")
        s_w13 = [sem(f"w13_loaded{b}") for b in range(3)]
        s_w2 = [sem(f"w2_loaded{b}") for b in range(3)]
        s_here13 = sem("w13_here")
        s_here2 = sem("w2_here")
        s_whi = sem("weights_high")
        s_wlo = sem("weights_low")
        s_oneh = sem("onehot_ready")
        s_id = sem("slot_terms")
        s_rid = sem("scatter_ids_ready")
        s_tick = sem("waits_taken")
        s_prep = sem("slots_found")
        s_slot = sem("slots_ready")
        s_xg = [sem(f"rows_gathered{b}") for b in range(2)]
        s_xgt = sem("rows_transposed")
        s_xgA = sem("rows_evac_act")
        s_xgD = sem("rows_evac_dve")
        s_e1 = sem("expert_mm1")
        s_esl = sem("expert_silu")
        s_eh = sem("expert_hidden")
        s_eht = sem("expert_hT")
        s_ehe = sem("expert_hT_evac")
        s_e2 = sem("expert_mm2")
        s_ey = sem("expert_rows")
        s_sc = [sem(f"rows_scattered{b}") for b in range(2)]
        s_fin = sem("experts_summed")
        s_fbc = sem("final_rows_loaded")
        s_x2 = sem("x2_ready")
        s_ssf = sem("x2_squares")
        s_res = sem("result_ready")
        s_irms = sem("x2_norm_ready")
        s_scaled = sem("result_scaled")
        s_out = sem("result_stored")
        s_rms = sem("rows_rms")
        s_cst = sem("conv_stats_out")
        s_rmsy = sem("mixer_rms")
        s_vec, s_gp = sem("vector_steps"), sem("gpsimd_steps")

        def pairs(eng, n_blocks, body):
            body(0)
            body(1)
            with eng.Fori(0, (PAIRS - 2) // RUN) as group:
                with eng.If(n_blocks > 2 * (RUN * group + 2) + 1):
                    with eng.Fori(0, RUN) as within:
                        j = RUN * group + within + 2
                        with eng.If(n_blocks > 2 * j + 1):
                            body(j)

        def reached(eng, s, n):
            if not (isinstance(n, int) and n == 0):
                eng.wait_ge(s, n)

        def new_expert(eng, i, act_on):
            e0 = eng.value_load(blk_row[0:1, bass.ds(i - 1, 1)], min_val=0, max_val=NE - 1)
            e = eng.value_load(blk_row[0:1, bass.ds(i, 1)], min_val=0, max_val=NE - 1)
            with eng.If(e > e0):
                act_on(e)

        def high_of(e):
            return (e % 2) * W13

        def third(e):
            return (e + 1) % 3

        def low_of(e):
            return third(e) * W13 + W_LO

        block = ctx.enter_context(nc.Block())

        @block.sync
        def _(q):
            def ada(n):
                if n >= RING:
                    q.wait_ge(s_gemv, n - RING + 1)
                q.dma_start(wada[:, n % RING], wada_v[:, :, 2 * D + n * PIECE:2 * D + (n + 1) * PIECE])\
                 .then_inc(s_ada[n % RING], 16)

            def bias_rows(m):
                if m:
                    q.wait_ge(s_rowst, 16 * m)
                q.dma_start(row[:].rearrange("o a n -> o (a n)"),
                            row_of(b_ada[2 * D + m * D:2 * D + (m + 1) * D])).then_inc(s_brow, 16)

            def w_in_chunk(m):
                if m >= 2:
                    q.wait_ge(s_cv, 6 * (m - 1))
                for j in range(3):
                    q.dma_start(win[:, m % 2, j], win_v[:, :, j * D_CONV + m * P:j * D_CONV + (m + 1) * P])\
                     .then_inc(s_win[m % 2], 16)

            q.dma_start(ccol[:], c.rearrange("b (p k) -> (b p) k", k=KC)).then_inc(s_cvec, 16)
            q.dma_start(x_tok[:, 0], x_v[:, 0]).then_inc(s_x[0], 16)
            for i in range(1, NT):
                q.dma_start(x_tok[:, i], x_v[:, i]).then_inc(s_x[i], 16)
            with nc.allow_non_contiguous_dma(reason="parameters, once"):
                q.dma_start(par[:, 0, :], lam_re).then_inc(s_s5in, 16)
                q.dma_start(par[:, 1, :], lam_im).then_inc(s_s5in, 16)
                q.dma_start(dtc[:, 0:1], log_dt.rearrange("(g o) -> g o", o=1)).then_inc(s_s5in, 16)
                for h, (t, u) in enumerate(((b_re, b_im), (b_im, b_re))):
                    q.dma_start(W0[0:S, h], t.rearrange("g p h -> p g h")).then_inc(s_s5in, 16)
                    q.dma_start(W0[S:2 * S, h], u.rearrange("g p h -> p g h")).then_inc(s_s5in, 16)
                for h, (t, u) in enumerate(((c_re, c_im), (c_im, c_re))):
                    for r in range(2):
                        q.dma_start(Cn[:, h, r, 0:S], t[r * 8:r * 8 + 8].rearrange("g h p -> (g h) p"))\
                           .then_inc(s_s5in, 16)
                        q.dma_start(Cn[:, h, r, S:2 * S], u[r * 8:r * 8 + 8].rearrange("g h p -> (g h) p"))\
                           .then_inc(s_s5in, 16)
            for n in range(4):
                h = slice((n % 2) * 512, (n % 2 + 1) * 512)
                q.dma_start(ada0[n // 2][:, :, h], wada_v[:, :, n * 512:(n + 1) * 512]).then_inc(s_ada0[n], 16)
            q.dma_start(wu[:], win_v[:, :, 3 * D_CONV:D_IN]).then_inc(s_wu, 16)
            with nc.allow_non_contiguous_dma(reason="parameters, once"):
                q.dma_start(bcol[:], b_ada[0:2 * D].rearrange("(a p k) -> p a k", p=P, k=KC)).then_inc(s_small, 16)
                q.dma_start(mcol[:, 2, :], g_mix.rearrange("(p k) -> p k", k=KC)).then_inc(s_small, 16)
                for w in range(3):
                    q.dma_start(cw[:, w, :], conv_w[w].rearrange("(m p) -> p m", p=P)).then_inc(s_small, 16)
                q.dma_start(cb[:], conv_b.rearrange("(m p) -> p m", p=P)).then_inc(s_small, 16)
                q.dma_start(gc[:], g_conv.rearrange("(m p) -> p m", p=P)).then_inc(s_small, 16)
                q.dma_start(gs[:], g_ssm.rearrange("(m p) -> p m", p=P)).then_inc(s_small, 16)
                q.dma_start(dskip[:], bcast(d_skip, P)).then_inc(s_small, 16)
                q.dma_start(bglu[:], bcast(b_glu, P)).then_inc(s_small, 16)
                q.dma_start(wglu[:], w_glu.rearrange("(k p) n -> p k n", p=P)).then_inc(s_small, 16)
            bias_rows(0)
            q.wait_ge(s_adac, 1)
            w_in_chunk(0)
            for n in range(RING):
                ada(n)
            w_in_chunk(1)
            for m in range(1, NM):
                for n in range(RING + PER_M * (m - 1), min(NP, RING + PER_M * m)):
                    ada(n)
                if m * PER_M < NP:
                    bias_rows(m)
                if m + 1 < NM:
                    w_in_chunk(m + 1)
                if m == 3:
                    q.wait_ge(s_ye, 4)
                    q.dma_start(wout[:], w_out.rearrange("(k p) n -> p k n", p=P)).then_inc(s_wout, 16)
            q.wait_ge(s_cv, 6 * NM)
            q.wait_ge(s_rowst, 16 * PER_M)
            for i in range(NT):
                q.dma_start(x1[:, i], x_v[:, i]).then_inc(s_x[i], 16)
            q.wait_ge(s_y2, 1)
            q.wait_ge(s_y3, 1)
            q.dma_start(gffn[:], bcast(g_ffn, P)).then_inc(s_bc, 16)
            q.wait_ge(s_yt, 4)
            for t, j in ((gate1, 2), (shift2, 3), (scale2, 4)):
                q.dma_start(t[:], modrow(j)).then_inc(s_bc, 16)
            q.dma_start(wr[:], w_router.rearrange("(p k) n -> p k n", k=KC)).then_inc(s_wr, 16)
            q.wait_ge(s_yg, NM)
            q.wait_ge(s_st, 1)
            q.dma_start(ws13[:, 0], ws1.rearrange("(p k) n -> p k n", k=KC)).then_inc(s_ws, 16)
            q.dma_start(ws13[:, 1], ws3.rearrange("(p k) n -> p k n", k=KC)).then_inc(s_ws, 16)
            q.dma_start(ws2t[:], ws2.rearrange("(p k) n -> p k n", k=FK)).then_inc(s_ws, 16)
            for i in range(NT):
                q.wait_ge(s_h2, i + 1)
                q.dma_start(h2_v[:, i], h2[:, i % 2]).then_inc(s_h2st[i % 2], 16)
            q.wait_ge(s_zr, 1)
            q.dma_start(h2_d[SEQ:ROWS, :], zrow[:]).then_inc(s_zst, 16)
            q.dma_start(ffn_d[SEQ:ROWS, :], zrow[:]).then_inc(s_zst, 16)
            q.wait_ge(s_op, NT)
            q.dma_start(rb[:], bcast(router_bias, P)).then_inc(s_small, 16)

            def pick(w, e):
                return w[bass.ds(e, 1), :, :].rearrange("e a b -> (e a) b")

            def load13(e, s):
                for j, w in enumerate((w1, w3)):
                    q.dma_start(w_raw[:, (s + 1) % 3, j], pick(w, e).rearrange("(p k) n -> p k n", k=KC))\
                     .then_inc(s_w13[s], 16)

            def load2(e, s):
                q.dma_start(w2t[:, (s + 1) % 3], pick(w2, e).rearrange("(p k) n -> p k n", k=FK))\
                 .then_inc(s_w2[s], 16)

            def here13(s, nth):
                q.wait_ge(s_w13[s], 32 * nth)
                q.sem_inc(s_here13, 1)

            def here2(s, nth):
                q.wait_ge(s_w2[s], 16 * nth)
                q.sem_inc(s_here2, 1)

            load13(0, 0)
            load2(0, 0)
            load13(1, 1)
            q.wait_ge(s_tab, 1)
            q.dma_start(blk_d.rearrange("(p o) -> p o", o=1), eblk_i[:]).then_inc(s_blk, 16)
            q.wait_ge(s_blk, 16)
            q.dma_start(blk_row[:], row_of(blk_d)).then_inc(s_blk, 16)
            here13(0, 1)
            here13(1, 1)
            here2(0, 1)
            q.wait_ge(s_m1, NT)
            load2(1, 1)
            q.wait_ge(s_m2, NT)
            load13(2, 2)
            load2(2, 2)
            here2(1, 1)

            q.wait_ge(s_route, 1)
            q.wait_ge(s_syst[1], 16 * 4)
            q.dma_start(gfin[:], bcast(g_final, P)).then_inc(s_fbc, 16)
            q.dma_start(gate2[:], modrow(5)).then_inc(s_fbc, 16)

            def blocks_up_to(e):
                return q.value_load(ends[0:1, bass.ds(e, 1)], min_val=1, max_val=MAX_BLOCKS)

            def next_load2(e, t, s):
                done = blocks_up_to(e - 3)
                q.wait_ge(s_e2, done)
                load2(e, s)
                here2((s - 1) % 3, t + 1 if s else t)

            def next_loads(t, s):
                e = 3 * t + s
                done = blocks_up_to(e - 3)
                q.wait_ge(s_e1, done)
                load13(e, s)
                here13((s - 1) % 3, t + 1 if s else t)
                if isinstance(e, int) and e == 3:
                    return
                next_load2(e - 1, t if s else t - 1, (s - 1) % 3)

            whole = NE // 3
            for s in range(3):
                next_loads(1, s)
            with q.Fori(2, whole) as t:
                for s in range(3):
                    next_loads(t, s)
            for s in range(NE % 3):
                next_loads(whole, s)
            final = NE - 1
            next_load2(final, final // 3, final % 3)
            here13(final % 3, final // 3 + 1)
            here2(final % 3, final // 3 + 1)
            q.wait_ge(s_fin, 1)
            for i in range(NT):
                q.dma_start(ffn[:, i], ffn_v[:, i]).then_inc(s_x[i], 16)
            for i in range(NT):
                q.wait_ge(s_res, i + 1)
                q.dma_start(out_v[:, i], res[:, i]).then_inc(s_out, 16)
            q.wait_ge(s_out, 16 * NT)

        @block.scalar
        def _(act):
            a = nc.scalar
            def root(j, i, width, done):
                a.activation(rs[:, j, i], ss[:, j, i], ACT.Sqrt, bias=eps[:, 0:1], scale=1.0 / width).then_inc(done, 1)

            act.wait_ge(s_consts, 1)
            act.wait_ge(s_cvec, 16)
            a.activation(sc[:], ccol[:], ACT.Silu).then_inc(s_silc, 1)
            for i in range(NT):
                act.wait_ge(s_x[i], 16)
                if i >= 1:
                    act.wait_ge(s_ssx, i)
                a.activation(hT[:, 7, :], x_tok[:, i], ACT.Square, accum_out=ss[:, 0, i:i + 1]).then_inc(s_ssx, 1)
                act.wait_ge(s_ssx, i + 1)
                root(0, slice(i, i + 1), D, s_rms)
            act.wait_ge(s_ssx, NT)
            for n in range(0, 16, 2):
                i, kq = n // 2, n % 2
                act.wait_ge(s_xt, n + 1)
                a.activation(hT[:, 4 * kq:4 * kq + 4, i * P:(i + 1) * P],
                             ps[:, n % 4, :].rearrange("p (k c) -> p k c", k=4), ACT.Copy).then_inc(s_xeA, 1)
            act.wait_ge(s_s5in, 16 * 15)
            a.activation(dtc[:, 1:2], dtc[:, 0:1], ACT.Exp).then_inc(s_s5a, 1)
            act.wait_ge(s_s5v, 1)
            a.activation(par[:, 3, :], par[:, 2, :], ACT.Exp).then_inc(s_s5a, 1)
            a.activation(par[:, 4, :], par[:, 2, :], ACT.Exp, scale=float(NT)).then_inc(s_s5a, 1)
            act.wait_ge(s_s5v, 2)
            a.activation(par[:, 7, :], par[:, 6, :], ACT.Sin).then_inc(s_s5a, 1)
            a.activation(par[:, 8, :], par[:, 6, :], ACT.Sin, scale=0.5).then_inc(s_s5a, 1)
            for n in range(4):
                act.wait_ge(s_row0, n + 1)
                a.activation(row0[:, n // 2, (n % 2) * 512:(n % 2 + 1) * 512], ps[0:1, 4 + n % 2, :], ACT.Copy)\
                 .then_inc(s_row0e, 1)

            def store_rows(m):
                act.wait_ge(s_row, PER_M * (m + 1))
                act.dma_start(row_of(mod_d[(2 + m) * D:(3 + m) * D]), row[:].rearrange("o a n -> o (a n)"))\
                   .then_inc(s_rowst, 16)

            act.wait_ge(s_a1, 1)
            act.wait_ge(s_xeA, 8)
            act.wait_ge(s_xeD, 8)
            for k in range(3):
                a.activation(hT[:, k, :], hT[:, k, :], ACT.Identity, bias=mcol[:, 0, k:k + 1],
                             scale=mcol[:, 3, k:k + 1]).then_inc(s_hA, 1)
            for n in range(4):
                act.wait_ge(s_u, n + 1)
                a.activation(U[:, :, 2 * n:2 * n + 2, :].rearrange("c g j h -> c j g h"),
                             ps[:, n, :].rearrange("c (j g h) -> c j g h", j=2, g=G), ACT.Copy).then_inc(s_ue, 1)
            def tables():
                act.wait_ge(s_Tm, 1)
                act.wait_ge(s_T0, 1)
                a.activation(T[:, NT - 1], ps[:, 4, 0:G * H].rearrange("p (g h) -> p g h", g=G), ACT.Copy)\
                 .then_inc(s_Te, 1)
                act.wait_ge(s_Te, 1)
                for i in range(NT - 1):
                    act.dma_start(T[0:(i + 1) * H, i], T[(NT - 1 - i) * H:P, NT - 1]).then_inc(s_Tsh, 16)
                for n in range(8):
                    act.wait_ge(s_Tm, n + 2)
                    dst = (ST, STs)[n // 4]
                    a.activation(dst[:, 4 * (n % 4):4 * (n % 4) + 4, :],
                                 ps[:, (5, 7, 4)[n % 3], :].rearrange("p (g c) -> p g c", g=4), ACT.Copy)\
                     .then_inc(s_Te, 1)

            def s5_ut(n):
                act.wait_ge(s_ut, n + 1)
                if n == 0:
                    act.wait_ge(s_Te, 9)
                    act.wait_ge(s_Q, 1)
                a.activation(UT[:], ps[:, 7, :].rearrange("p (g c) -> p g c", g=4), ACT.Copy).then_inc(s_ute, 1)

            def conv_gate(m, half):
                act.wait_ge(s_cv, 6 * m + 2 * half + 1)
                if m or half:
                    act.wait_ge(s_z, 2 * m + half)
                a.activation(cs[:], ps[:, (6 * m + 2 * half) % 4, :], ACT.Copy).then_inc(s_ce, 1)

            for m in range(NM):
                conv_gate(m, 0)
                if m == 2:
                    s5_ut(2)
                conv_gate(m, 1)
                if m == 0:
                    tables()
                if m < 3:
                    s5_ut((0, 1, 3)[m])
                if m == 4:
                    for n in range(4):
                        act.wait_ge(s_gt, n + 1)
                        a.activation(ys[:, :, 2 * n * P:2 * (n + 1) * P].rearrange("p k (i c) -> p i k c", i=2),
                                     ps[:, 4 + n % 2, :].rearrange("p (i k c) -> p i k c", i=2, k=2),
                                     ACT.Copy).then_inc(s_gte, 1)
                if m == 5:
                    for n in range(4):
                        act.wait_ge(s_gb, n + 1)
                        a.activation(glu[:, 2 * n:2 * n + 2, :], glu[:, 2 * n:2 * n + 2, :],
                                     ACT.Sigmoid).then_inc(s_gsg, 1)
                act.wait_ge(s_y, 2 * (m + 1))
                if m:
                    act.wait_ge(s_sqs, m)
                a.activation(sq[:], yc[:, m, :], ACT.Square).then_inc(s_sq, 1)
                act.wait_ge(s_sq, m + 1)
                a.activation(yc[:, m, :], yc[:, m, :], ACT.Copy, scale=gc[:, m:m + 1]).then_inc(s_yg, 1)
                if m * PER_M < NP:
                    store_rows(m)
                if m == 3:
                    act.wait_ge(s_ye, 4)
                    a.activation(y2[:].rearrange("c i (g h) -> c g i h", h=H), y[:], ACT.Gelu_apprx_tanh).then_inc(s_gel, 1)
            act.wait_ge(s_y2, 1)
            for i in range(NT):
                a.activation(glu[:, i, :], y2[:, i, :], ACT.Square,
                             accum_out=ss[:, 2, i:i + 1]).then_inc(s_ss2, 1)
            act.wait_ge(s_ss2, NT)
            root(2, slice(0, NT), D_SSM, s_rmsy)
            act.wait_ge(s_cst, 1)
            root(1, slice(0, NT), D_CONV, s_rmsy)
            for n in range(4):
                act.wait_ge(s_yt, n + 1)
                for k in range(2):
                    a.activation(ys[:, k, 2 * n * P:2 * (n + 1) * P].rearrange("p (i c) -> p i c", i=2),
                                 ps[:, 4 + n % 2, :].rearrange("p (i k c) -> p i k c", i=2, k=2)[:, :, k, :],
                                 ACT.Copy, scale=gs[:, k:k + 1]).then_inc(s_yte, 1)

            def h2_evac(i):
                act.wait_ge(s_h2t, i + 1)
                for kq in range(2):
                    a.activation(h2T[:, 4 * kq:4 * kq + 4, i * P:(i + 1) * P],
                                 ps[:, 4 + kq, :].rearrange("p (k c) -> p k c", k=4), ACT.Copy).then_inc(s_h2e, 1)

            for i in range(NT):
                act.wait_ge(s_x1, i + 1)
                if i:
                    act.wait_ge(s_ssr, i)
                a.activation(junk[:], x1[:, i], ACT.Square, accum_out=ss[:, 3, i:i + 1]).then_inc(s_ssr, 1)
                act.wait_ge(s_ssr, i + 1)
                root(3, slice(i, i + 1), D, s_rms)
                if i:
                    h2_evac(i - 1)
            h2_evac(NT - 1)
            for half in range(2):
                act.wait_ge(s_lg, half + 1)
                act.wait_ge(s_ssr, NT)
                a.activation(lgT[:, half * 512:(half + 1) * 512], ps[0:NE, 6 + half, :], ACT.Copy).then_inc(s_lge, 1)
            act.wait_ge(s_lg, 3)
            act.wait_ge(s_h2st[0], 16 * 4)
            act.wait_ge(s_h2st[1], 16 * 4)
            a.activation(sig[:], ps[:, 3, :].rearrange("c (i e) -> c i e", i=NT), ACT.Sigmoid).then_inc(s_sg, 1)
            def weights_high(e):
                act.wait_ge(s_here13, e + 1)
                raw = w_raw[:].rearrange("p q a k n -> p (q a k n)")
                for n in range(4):
                    a.activation(w_parts[:, bass.ds(high_of(e) + n * (W13 // 4), W13 // 4)],
                                 raw[:, bass.ds(low_of(e) - W_LO + n * (W13 // 4), W13 // 4)], ACT.Copy)\
                     .then_inc(s_whi, 1)

            for i in range(NT + 1):
                if i == NT:
                    weights_high(0)
                if i < NT:
                    act.wait_ge(s_m1, i + 1)
                    if i >= 2:
                        act.wait_ge(s_hd, i - 1)
                    a.activation(sil[i % 2][:], ps[:, i % 2, 0:FE], ACT.Silu).then_inc(s_sl, 1)
                if i:
                    t = i - 1
                    act.wait_ge(s_m2, t + 1)
                    if t >= 2:
                        act.wait_ge(s_syst[t % 2], 16 * (t // 2))
                    a.activation(shy[t % 2][:].rearrange("c (n f) -> c n f", n=2),
                                 ps[:, 4 + 2 * (t % 2):6 + 2 * (t % 2), :], ACT.Copy).then_inc(s_sy, 1)
                    act.wait_ge(s_sy, t + 1)
                    act.dma_start(ffn_v[:, t], shy[t % 2][:]).then_inc(s_syst[t % 2], 16)

            n_blocks = act.value_load(nblk[0:1, 0:1], min_val=NE, max_val=MAX_BLOCKS)

            def turned_high(i, b):
                reached(act, s_xgt, i + 1)
                for kq in range(2):
                    a.activation(xgh[b][:, 4 * kq:4 * kq + 4, :],
                                 ps[:, 4 + kq, :].rearrange("p (k c) -> p k c", k=4), ACT.Copy).then_inc(s_xgA, 1)

            def rows_out(b):
                a.activation(yo[b][:].rearrange("c (n f) -> c n f", n=2), ps[:, 6:8, :], ACT.Copy).then_inc(s_ey, 1)

            def silu(b):
                a.activation(sil[b][:], ps[:, b, 0:FE], ACT.Silu).then_inc(s_esl, 1)

            def hidden_turned(b):
                a.activation(hidT[b][:].rearrange("p k c -> p (k c)"), ps[:, 2, 2 * b * P:2 * (b + 1) * P],
                             ACT.Copy).then_inc(s_ehe, 1)

            turned_high(0, 0)
            new_expert(act, 1, weights_high)

            def pair(j):
                for i, b, stored in ((2 * j + 1, 1, j - 1), (2 * j + 2, 0, j)):
                    if not (isinstance(i, int) and i == 1):
                        reached(act, s_eht, i - 1)
                        hidden_turned(b)
                    reached(act, s_e1, i)
                    silu(1 - b)
                    turned_high(i, b)
                    new_expert(act, i + 1, weights_high)
                    if isinstance(i, int) and i == 1:
                        continue
                    reached(act, s_e2, i - 1)
                    reached(act, s_sc[b], 16 * stored)
                    rows_out(b)

            pairs(act, n_blocks, pair)
            last = (n_blocks // 2) * 2
            act.wait_ge(s_e1, last + 1)
            silu(0)
            act.wait_ge(s_eht, last)
            hidden_turned(1)
            act.wait_ge(s_eht, last + 1)
            hidden_turned(0)
            act.wait_ge(s_e2, last)
            act.wait_ge(s_sc[0], 16 * (n_blocks // 2))
            rows_out(1)
            act.wait_ge(s_e2, last + 1)
            rows_out(0)
            for i in range(NT):
                act.wait_ge(s_x2, i + 1)
                if i:
                    act.wait_ge(s_ssf, i)
                a.activation(shy[0][:], x1[:, i], ACT.Square, accum_out=ss[:, 4, i:i + 1]).then_inc(s_ssf, 1)
                act.wait_ge(s_ssf, i + 1)
                root(4, slice(i, i + 1), D, s_rms)
                act.wait_ge(s_irms, i + 1)
                a.activation(res[:, i], x1[:, i], ACT.Copy, scale=rs[:, 4, i:i + 1]).then_inc(s_scaled, 1)

        @block.tensor
        def _(pe):
            t = nc.tensor
            pe.wait_ge(s_consts, 1)
            for n in range(16):
                i, kq = n // 2, n % 2
                pe.wait_ge(s_xn, i + 1)
                if n >= 4:
                    pe.wait_ge(s_xeA if n % 2 == 0 else s_xeD, n // 2 - 1)
                for k in range(4):
                    mm = t.transpose(ps[:, n % 4, k * P:(k + 1) * P],
                                     x_tok[:, i].rearrange("c (p k) -> c k p", k=KC)[:, 4 * kq + k, :], ident[:])
                mm.then_inc(s_xt, 1)

            def first_row(n):
                pe.wait_ge(s_ada0[n], 16)
                if n >= 2:
                    pe.wait_ge(s_row0e, n - 1)
                for k in range(KC):
                    mm = t.matmul(ps[0:1, 4 + n % 2, :], sc[:, k:k + 1],
                                  ada0[n // 2][:, k, (n % 2) * 512:(n % 2 + 1) * 512],
                                  start=(k == 0), stop=(k == KC - 1))
                mm.then_inc(s_row0, 1)

            pe.wait_ge(s_silc, 1)
            first_row(0)
            first_row(1)

            pe.wait_ge(s_s5v, 3)
            for j in range(7):
                mm = t.transpose(ps[:, 7, j * G:(j + 1) * G], pdup[:, j, :], ident[0:G, 0:G])
            mm.then_inc(s_pt, 1)
            pe.wait_ge(s_cneg, 2)
            for h in range(2):
                for r in range(2):
                    mm = t.transpose(ps[:, 6, (2 * h + r) * P:(2 * h + r + 1) * P], Cn[:, h, r, :], ident[:])
            mm.then_inc(s_pt, 1)
            def ada_row(n):
                pe.wait_ge(s_gemv, n + 1)
                if n:
                    pe.wait_ge(s_row, n)
                t.matmul(ps[0:1, 6, 0:PIECE], ones[:, 0:1], acc[:], start=True, stop=True).then_inc(s_adar, 1)

            first_row(2)
            first_row(3)
            pe.wait_ge(s_C, 1)
            for j in range(2):
                pe.wait_ge(s_row0e, 2 * j + 2)
                for f in range(KC):
                    mm = t.matmul(ps[:, 6, j * KC + f:j * KC + f + 1],
                                  row0[:, j].rearrange("c (p f) -> c f p", f=KC)[:, f, :], ones[0:1, 0:1],
                                  start=True, stop=True)
            mm.then_inc(s_adac, 1)
            pe.wait_ge(s_hA, 3)
            pe.wait_ge(s_hD, 5)
            pe.wait_ge(s_wu, 16)
            for j in range(NT):
                for k in range(KC):
                    mm = t.matmul(ps[:, j // 2, (j % 2) * D_SSM:(j % 2 + 1) * D_SSM], hT[:, k, j * P:(j + 1) * P],
                                  wu[:, k, :], start=(k == 0), stop=(k == KC - 1))
                if j % 2:
                    mm.then_inc(s_u, 1)
            def tables():
                pe.wait_ge(s_V, 1)
                pe.wait_ge(s_pe, 1)
                pe.wait_ge(s_row, 2)
                for g in range(G):
                    mm = t.matmul(ps[:, 4, g * H:(g + 1) * H], V[:, g, 0:NT, :].rearrange("p m h -> p (m h)"),
                                  C0[:, 0, g, :], start=True, stop=True)
                mm.then_inc(s_Tm, 1)
                for n in range(8):
                    if n >= 2:
                        pe.wait_ge(s_Te, n - 1)
                    for gq in range(4):
                        g = 4 * (n % 4) + gq
                        src = V[:, g, 0:NT, :] if n < 4 else Vs[:, g, :, :]
                        mm = t.transpose(ps[:, (5, 7, 4)[n % 3], gq * P:(gq + 1) * P],
                                         src.rearrange("p m h -> p (m h)"), ident[:])
                    mm.then_inc(s_Tm, 1)
                pe.wait_ge(s_Te, 9)

            def conv_group(m, n):
                half, j = (n - 4, 0) if n >= 4 else (n // 2, 1 + n % 2)
                if m == 0 and n < 4:
                    pe.wait_ge(s_ue, 4)
                elif n == 0:
                    pe.wait_ge(s_ce, 2 * m)
                elif n == 1:
                    pe.wait_ge(s_z, 2 * m)
                elif n in (2, 3):
                    pe.wait_ge(s_y, 2 * m - 3 + n)
                elif n == 4:
                    pe.wait_ge(s_ce, 2 * m + 1)
                else:
                    pe.wait_ge(s_z, 2 * m + 1)
                for k in range(KC):
                    mm = t.matmul(ps[:, (6 * m + n) % 4, :], win[:, m % 2, j, k, :],
                                  hT[:, k, half * 512:(half + 1) * 512], start=(k == 0), stop=(k == KC - 1))
                mm.then_inc(s_cv, 1)

            def s5_turn(n):
                if n:
                    pe.wait_ge(s_ye, n)
                for gq in range(4):
                    mm = t.transpose(ps[:, 7, gq * P:(gq + 1) * P],
                                     U[:, 4 * n + gq].rearrange("c j h -> c (j h)"), ident[:])
                mm.then_inc(s_ut, 1)

            def s5_in(n):
                pe.wait_ge(s_ute, n + 1)
                if n:
                    pe.wait_ge(s_r, n)
                for gq in range(4):
                    g = 4 * n + gq
                    t.matmul(ps[:, 4, gq * P:(gq + 1) * P], ST[:, g, :], UT[:, gq, :], start=True, stop=True)
                    mm = t.matmul(ps[:, 5, gq * P:(gq + 1) * P], STs[:, g, :], UT[:, gq, :], start=True, stop=True)
                mm.then_inc(s_s, 1)

            def s5_out(n):
                pe.wait_ge(s_r, n + 1)
                pe.wait_ge(s_Tsh, 16 * (NT - 1))
                for gq in range(4):
                    g = 4 * n + gq
                    o = ps[:, 7, gq * P:(gq + 1) * P]
                    t.matmul(o, UT[:, gq, :], T[:, :, g, :], start=True, stop=False)
                    t.matmul(o, R1[:, gq, 0:P], Q[:, g].rearrange("p i h -> p (i h)"), start=False, stop=False)
                    mm = t.matmul(o, R2[:, gq, 0:P], Qs[:, g].rearrange("p i h -> p (i h)"), start=False, stop=True)
                mm.then_inc(s_ym, 1)

            for m in range(NM):
                pe.wait_ge(s_win[m % 2], 48 * (m // 2 + 1))
                pieces = m * PER_M < NP
                s5_steps = {(0, 4): (s5_turn, 0), (0, 5): (s5_in, 0),
                            (1, 1): (s5_out, 0), (1, 2): (s5_turn, 1), (1, 3): (s5_in, 1), (1, 5): (s5_out, 1),
                            (2, 0): (s5_turn, 2), (2, 1): (s5_in, 2), (2, 3): (s5_out, 2), (2, 4): (s5_turn, 3),
                            (2, 5): (s5_in, 3), (3, 1): (s5_out, 3)}
                for n in range(6):
                    conv_group(m, n)
                    if pieces and n in (1, 3, 4, 5):
                        ada_row(PER_M * m + {1: 0, 3: 1, 4: 2, 5: 3}[n])
                    if (m, n) == (0, 3):
                        tables()
                    if (m, n) in s5_steps:
                        s5_step, quad = s5_steps[m, n]
                        s5_step(quad)
                    if (m, n) == (4, 3):
                        pe.wait_ge(s_gel, 1)
                        for n4 in range(4):
                            if n4 >= 2:
                                pe.wait_ge(s_gte, n4 - 1)
                            for q4 in range(4):
                                i, k = 2 * n4 + q4 // 2, q4 % 2
                                mm = t.transpose(ps[:, 4 + n4 % 2, q4 * P:(q4 + 1) * P],
                                                 y2[:, i, k * P:(k + 1) * P], ident[:])
                            mm.then_inc(s_gt, 1)
                if m == 4:
                    pe.wait_ge(s_gte, 4)
                    pe.wait_ge(s_row, NP)
                    for n in range(4):
                        for i in (2 * n, 2 * n + 1):
                            for k in range(2):
                                mm = t.matmul(ps[:, (4, 5, 7, 6)[n], (i % 2) * D_SSM:(i % 2 + 1) * D_SSM],
                                              ys[:, k, i * P:(i + 1) * P], wglu[:, k, :],
                                              start=(k == 0), stop=(k == 1))
                        mm.then_inc(s_gm, 1)
            def project(i, chunks):
                for n in range(2):
                    for k in chunks:
                        lhs = yc[:, k, i * P:(i + 1) * P] if k < NM else ys[:, k - NM, i * P:(i + 1) * P]
                        mm = t.matmul(ps[:, 2 * (i % 2) + n, :], lhs, wout[:, k, n * 512:(n + 1) * 512],
                                      start=(k == 0), stop=(k == KC - 1))
                return mm

            pe.wait_ge(s_wout, 16)
            pe.wait_ge(s_z, 2 * NM)
            pe.wait_ge(s_yg, NM - 1)
            project(0, range(NM - 1))
            pe.wait_ge(s_sqs, NM)
            pe.wait_ge(s_gb, 4)
            for i in range(NT):
                mm = t.matmul(ps[:, 6, i:i + 1], sqsum[:, i * P:(i + 1) * P], ones[:, 0:1], start=True, stop=True)
            mm.then_inc(s_st, 1)
            pe.wait_ge(s_y, 2 * NM)
            project(1, range(NM - 1))
            pe.wait_ge(s_y3, 1)
            for n in range(4):
                if n >= 2:
                    pe.wait_ge(s_yte, 2 * (n - 1))
                for q4 in range(4):
                    i, k = 2 * n + q4 // 2, q4 % 2
                    mm = t.transpose(ps[:, 4 + n % 2, q4 * P:(q4 + 1) * P], y2[:, i, k * P:(k + 1) * P], ident[:])
                mm.then_inc(s_yt, 1)
            pe.wait_ge(s_yg, NM)
            pe.wait_ge(s_yte, 8)

            def h2_transpose(i):
                pe.wait_ge(s_h2, i + 1)
                if i:
                    pe.wait_ge(s_h2e, 2 * i)
                for k in range(KC):
                    mm = t.transpose(ps[:, 4 + k // 4, (k % 4) * P:(k % 4 + 1) * P],
                                     h2[:, i % 2].rearrange("c (p k) -> c k p", k=KC)[:, k, :], ident[:])
                mm.then_inc(s_h2t, 1)

            for i in range(NT):
                if i >= 2:
                    pe.wait_ge(s_x1, i - 1)
                project(i, range(NM - 1, KC) if i < 2 else range(KC)).then_inc(s_op, 1)
                if i:
                    h2_transpose(i - 1)
            pe.wait_ge(s_wr, 16)
            for half in range(2):
                if half:
                    h2_transpose(NT - 1)
                pe.wait_ge(s_h2e, NT * (half + 1))
                for k in range(KC):
                    mm = t.matmul(ps[0:NE, 6 + half, :], wr[:, k, :], h2T[:, k, half * 512:(half + 1) * 512],
                                  start=(k == 0), stop=(k == KC - 1))
                mm.then_inc(s_lg, 1)
            pe.wait_ge(s_ws, 48)

            def find_slots(i, b):
                pe.wait_ge(s_oneh, i * 2 + 2)
                for k in range(NT):
                    mm = t.matmul(ps[:, 3, 8 * b:8 * b + 6], oneh[b][:, k, :], wv[b][:, k, :],
                                  start=(k == 0), stop=(k == NT - 1))
                mm.then_inc(s_prep, 1)

            def shared_turn(i):
                pe.wait_ge(s_hd, i + 1)
                if i:
                    pe.wait_ge(s_hte, i)
                for k in range(FK):
                    mm = t.transpose(ps[:, 2, k * P:(k + 1) * P],
                                     hid[i % 2][:].rearrange("c (p k) -> c k p", k=FK)[:, k, :], ident[:])
                mm.then_inc(s_ht, 1)

            for i in range(NT + 1):
                if i < NT:
                    if i >= 2:
                        pe.wait_ge(s_hd, i - 1)
                    for k in range(KC):
                        mm = t.matmul(ps[:, i % 2, :], h2T[:, k, i * P:(i + 1) * P], ws13[:, :, k, :],
                                      start=(k == 0), stop=(k == KC - 1))
                        if i and k == KC - 3:
                            shared_turn(i - 1)
                    mm.then_inc(s_m1, 1)
                if i == 0:
                    pe.wait_ge(s_x1, NT)
                    pe.wait_ge(s_lge, 2)
                    for n in range(NT):
                        mm = t.transpose(ps[:, 3, n * NE:(n + 1) * NE], lgT[:, n * P:(n + 1) * P], ident[0:NE, 0:NE])
                    mm.then_inc(s_lg, 1)
                if i:
                    b = (i - 1) % 2
                    if i == NT:
                        shared_turn(i - 1)
                    pe.wait_ge(s_hte, i)
                    if i >= 3:
                        pe.wait_ge(s_sy, i - 2)
                    for n in range(2):
                        for k in range(FK):
                            mm = t.matmul(ps[:, 4 + 2 * b + n, :], hidT[b][:, k, :], ws2t[:, k, n * 512:(n + 1) * 512],
                                          start=(k == 0), stop=(k == FK - 1))
                    mm.then_inc(s_m2, 1)
                if i == 3:
                    pe.wait_ge(s_sel, 1)
                    t.matmul(ps[:, 3, :], tri[:], selb[:].rearrange("c i e -> c (i e)"), start=True, stop=True)\
                     .then_inc(s_rank, 1)
                if i == 4:
                    pe.wait_ge(s_ranke, 1)
                    t.matmul(ps[:, 3, :], onesb[:], selb[:].rearrange("c i e -> c (i e)"), start=True, stop=True)\
                     .then_inc(s_cnt, 1)
                if i == 6:
                    pe.wait_ge(s_route, 1)
                    find_slots(0, 0)
                if i == 7:
                    pe.wait_ge(s_slot, 1)
                    find_slots(1, 1)

            def rows_in(b):
                for k in range(KC):
                    mm = t.transpose(ps[:, 4 + k // 4, (k % 4) * P:(k % 4 + 1) * P],
                                     xg[b][:].rearrange("c (p k) -> c k p", k=KC)[:, k, :], ident[:])
                mm.then_inc(s_xgt, 1)

            def expert(i):
                return pe.value_load(blk_row[0:1, bass.ds(i, 1)], min_val=0, max_val=NE - 1)

            def product1(e, b):
                pe.wait_ge(s_wlo, (e + 1) * 4)
                high, low = (w_parts[:, bass.ds(start, W13)].rearrange("p (a k n) -> p a k n", a=2, k=KC)
                             for start in (high_of(e), low_of(e)))
                for k in range(KC):
                    t.matmul(ps[:, b, :], xgh[b][:, k, :], high[:, :, k, :], start=(k == 0), stop=False)
                    t.matmul(ps[:, b, :], xgh[b][:, k, :], low[:, :, k, :], start=False, stop=False)
                    mm = t.matmul(ps[:, b, :], xgl[b][:, k, :], high[:, :, k, :], start=False, stop=(k == KC - 1))
                mm.then_inc(s_e1, 1)

            def hidden_turn(b):
                for k in range(FK):
                    mm = t.transpose(ps[:, 2, (2 * b + k) * P:(2 * b + k + 1) * P],
                                     hid[b][:].rearrange("c (p k) -> c k p", k=FK)[:, k, :], ident[:])
                mm.then_inc(s_eht, 1)

            def product2(e, b):
                w = w2t[:].rearrange("p q k n -> p (q k) n")
                pe.wait_ge(s_here2, e + 1)
                for n in range(2):
                    for k in range(FK):
                        mm = t.matmul(ps[:, 6 + n, :], hidT[b][:, k, :],
                                      w[:, bass.ds(third(e) * FK + k, 1), n * 512:(n + 1) * 512],
                                      start=(k == 0), stop=(k == FK - 1))
                mm.then_inc(s_e2, 1)

            pe.wait_ge(s_slot, 2)
            find_slots(2, 0)
            pe.wait_ge(s_sy, NT - 1)
            pe.wait_ge(s_xg[0], 16)
            rows_in(0)
            pe.wait_ge(s_xgD, 2)
            product1(0, 0)
            n_blocks = pe.value_load(nblk[0:1, 0:1], min_val=NE, max_val=MAX_BLOCKS)

            def pair(j):
                for i, b, mine in ((2 * j + 1, 1, j + 1), (2 * j + 2, 0, j + 2)):
                    first = isinstance(i, int) and i == 1
                    e = expert(i)
                    if not first:
                        e_before = expert(i - 2)
                        reached(pe, s_eh, i - 1)
                        reached(pe, s_ehe, i - 2)
                        hidden_turn(b)
                    reached(pe, s_xg[b], 16 * mine)
                    rows_in(b)
                    reached(pe, s_slot, i + 2)
                    find_slots(i + 2, b)
                    if not first:
                        reached(pe, s_ehe, i - 1)
                        reached(pe, s_ey, i - 2)
                        if isinstance(i, int) and i == 2:
                            pe.wait_ge(s_sy, NT)
                        product2(e_before, b)
                    reached(pe, s_xgD, 2 * i + 2)
                    product1(e, b)

            pairs(pe, n_blocks, pair)
            last = (n_blocks // 2) * 2
            e, e_last = expert(last - 1), expert(last)
            pe.wait_ge(s_eh, last)
            hidden_turn(1)
            pe.wait_ge(s_ehe, last)
            pe.wait_ge(s_eh, last + 1)
            hidden_turn(0)
            product2(e, 1)
            pe.wait_ge(s_ehe, last + 1)
            pe.wait_ge(s_ey, last)
            product2(e_last, 0)

        @block.vector
        def _(dve):
            v = nc.vector
            step = Steps(dve, s_vec)

            tt, ts = v.tensor_tensor, v.tensor_scalar
            one = lambda i: slice(i, i + 1)
            for i in range(NT):
                dve.wait_ge(s_rms, i + 1)
                step(v.reciprocal(rs[:, 0, one(i)], rs[:, 0, one(i)]))
                ts(x_tok[:, i], x_tok[:, i], rs[:, 0, one(i)], None, ALU.mult).then_inc(s_xn, 1)
            dve.wait_ge(s_ssx, NT)
            for n in range(1, 16, 2):
                i, kq = n // 2, n % 2
                dve.wait_ge(s_xt, n + 1)
                v.tensor_copy(hT[:, 4 * kq:4 * kq + 4, i * P:(i + 1) * P],
                              ps[:, n % 4, :].rearrange("p (k c) -> p k c", k=4)).then_inc(s_xeD, 1)


            R = lambda j: par[:, j, :]
            dve.wait_ge(s_s5a, 1)
            tt(R(2), R(0), dtc[:, 1:2].to_broadcast([G, S]), ALU.mult).then_inc(s_s5v, 1)
            step(tt(R(5), R(1), dtc[:, 1:2].to_broadcast([G, S]), ALU.mult))
            step(ts(R(6), R(5), 1.0 / (2 * 3.141592653589793), ROUND, ALU.mult, ALU.add))
            step(ts(R(6), R(6), ROUND, None, ALU.subtract))
            step(v.scalar_tensor_tensor(R(5), R(6), -TWO_PI_HI, R(5), ALU.mult, ALU.add))
            step(v.scalar_tensor_tensor(R(5), R(6), -TWO_PI_MID, R(5), ALU.mult, ALU.add))
            step(v.scalar_tensor_tensor(R(5), R(6), -TWO_PI_LO, R(5), ALU.mult, ALU.add))
            ts(R(6), R(5), PI, -PI, ALU.min, ALU.max).then_inc(s_s5v, 1)
            dve.wait_ge(s_s5a, 5)
            step(tt(R(9), R(8), R(8), ALU.mult))
            step(ts(R(9), R(9), -2.0, 1.0, ALU.mult, ALU.add))
            step.run(tt(R(10), R(3), R(9), ALU.mult))
            step.run(tt(R(11), R(3), R(7), ALU.mult))
            step.run(tt(R(12), R(0), R(0), ALU.mult))
            step.run(tt(R(13), R(1), R(1), ALU.mult))
            step.settle()
            step.run(tt(R(12), R(12), R(13), ALU.add))
            step.run(ts(R(14), R(10), -1.0, None, ALU.add))
            step.settle()
            step.run(v.reciprocal(R(13), R(12)))
            step.run(tt(R(15), R(14), R(0), ALU.mult))
            step.run(tt(R(16), R(11), R(1), ALU.mult))
            step.run(tt(R(17), R(11), R(0), ALU.mult))
            step.run(tt(R(18), R(14), R(1), ALU.mult))
            step.settle()
            step.run(tt(R(15), R(15), R(16), ALU.add))
            step.run(tt(R(17), R(17), R(18), ALU.subtract))
            step.settle()
            step.run(tt(R(15), R(15), R(13), ALU.mult))
            step.run(tt(R(17), R(17), R(13), ALU.mult))
            cur = (9, 7)
            for n in range(3):
                nxt = (19, 20) if n % 2 == 0 else (21, 22)
                step.run(tt(R(23), R(cur[1]), R(cur[1]), ALU.mult))
                step.run(tt(R(nxt[1]), R(cur[0]), R(cur[1]), ALU.mult))
                step.settle()
                step.run(ts(R(nxt[0]), R(23), -2.0, 1.0, ALU.mult, ALU.add))
                step.run(ts(R(nxt[1]), R(nxt[1]), 2.0, None, ALU.mult))
                step.settle()
                cur = nxt
            for j, r in enumerate((10, 11, 15, 17, cur[0], cur[1], 4)):
                step.run(v.tensor_copy(pdup[:, j, 0:S], R(r)))
                step.run(v.tensor_copy(pdup[:, j, S:2 * S], R(r)))
            step.settle()
            ts(dtc[:, 2:3], dtc[:, 1:2], 1.0, None, ALU.mult).then_inc(s_s5v, 1)
            ts(Cn[:, 0, :, S:2 * S], Cn[:, 0, :, S:2 * S], -1.0, None, ALU.mult).then_inc(s_cneg, 1)
            ts(Cn[:, 1, :, :], Cn[:, 1, :, :], -1.0, None, ALU.mult).then_inc(s_cneg, 1)
            dve.wait_ge(s_pt, 1)
            v.tensor_copy(sp[:].rearrange("p a g -> p (a g)"), ps[:, 7, 0:7 * G]).then_inc(s_pe, 1)
            dve.wait_ge(s_pt, 2)
            v.tensor_copy(C0[:].rearrange("p a g h -> p (a g h)"), ps[:, 6, :]).then_inc(s_C, 1)

            def weighted(o, w, last):
                for k in range(KC):
                    if k == 0:
                        ins = ts(o, w[:, 0, :], sc[:, 0:1], None, ALU.mult)
                    else:
                        ins = v.scalar_tensor_tensor(o, w[:, k, :], sc[:, one(k)], o, ALU.mult, ALU.add)
                    if k < KC - 1:
                        step(ins)
                    else:
                        ins.then_inc(last, 1)

            def partials(n):
                dve.wait_ge(s_ada[n % RING], 16 * (n // RING + 1))
                if n:
                    dve.wait_ge(s_adar, n)
                weighted(acc[:], wada[:, n % RING], s_gemv)

            def add_row(n):
                dve.wait_ge(s_adar, n + 1)
                dve.wait_ge(s_brow, 16 * (n // PER_M + 1))
                tt(row[:, n % PER_M, :], row[:, n % PER_M, :], ps[0:1, 6, 0:PIECE], ALU.add).then_inc(s_row, 1)

            dve.wait_ge(s_silc, 1)
            dve.wait_ge(s_small, 16 * 11)
            dve.wait_ge(s_adac, 1)
            step(tt(mcol[:, 0:2, :], ps[:, 6, 0:2 * KC].rearrange("p (a k) -> p a k", a=2), bcol[:], ALU.add))
            v.scalar_tensor_tensor(mcol[:, 3, :], mcol[:, 1, :], 1.0, mcol[:, 2, :], ALU.add, ALU.mult)\
             .then_inc(s_a1, 1)
            dve.wait_ge(s_a1, 1)
            dve.wait_ge(s_xeA, 8)
            dve.wait_ge(s_xeD, 8)
            for k in range(3, 8):
                ts(hT[:, k, :], hT[:, k, :], mcol[:, 3, one(k)], mcol[:, 0, one(k)], ALU.mult, ALU.add)\
                 .then_inc(s_hD, 1)

            tmp = lambda j: ztmp[:, j, :].rearrange("p (g h) -> p g h", g=G)
            wide = lambda ap: ap.unsqueeze(2).to_broadcast([P, G, H])
            dve.wait_ge(s_pe, 1)
            dve.wait_ge(s_C, 1)
            for i in range(NT):
                a_, b_ = (C0[:, 0], C0[:, 1]) if i == 0 else (Q[:, :, i - 1, :], Qs[:, :, i - 1, :])
                step.run(tt(tmp(0), a_, wide(sp[:, 0]), ALU.mult))
                step.run(tt(tmp(1), b_, wide(sp[:, 1]), ALU.mult))
                step.run(tt(tmp(2), b_, wide(sp[:, 0]), ALU.mult))
                step.run(tt(tmp(3), a_, wide(sp[:, 1]), ALU.mult))
                step.settle()
                step.run(tt(Q[:, :, i, :], tmp(0), tmp(1), ALU.add))
                step.run(tt(Qs[:, :, i, :], tmp(2), tmp(3), ALU.subtract))
                step.settle()
            step(v.memset(z[:, 0:2, 0:1], 0.0))
            v.tensor_copy(dtc[:, 3:4], dtc[:, 2:3]).then_inc(s_Q, 1)

            def conv_z(m, half):
                dve.wait_ge(s_ce, 2 * m + half + 1)
                dve.wait_ge(s_cv, 6 * m + 2 * half + 2)
                tt(z[:, 2 + 4 * half:6 + 4 * half, :].rearrange("p i c -> p (i c)"), cs[:],
                   ps[:, (6 * m + 2 * half + 1) % 4, :], ALU.mult).then_inc(s_z, 1)

            def conv(m, row_turn):
                if m == 0:
                    dve.wait_ge(s_V, 1)
                    dve.wait_ge(s_Te, 9)
                dve.wait_ge(s_z, 2 * m + 2)
                step(v.tensor_copy(z[:, 0:2, 1:P], z[:, NT:NT + 2, 0:P - 1]))
                o = yc[:, m, :].rearrange("p (i c) -> p i c", i=NT)
                step(ts(o, z[:, 2:2 + NT, :], cw[:, 2, one(m)], cb[:, one(m)], ALU.mult, ALU.add))
                step(v.scalar_tensor_tensor(o, z[:, 1:1 + NT, :], cw[:, 1, one(m)], o, ALU.mult, ALU.add))
                step(v.scalar_tensor_tensor(o, z[:, 0:NT, :], cw[:, 0, one(m)], o, ALU.mult, ALU.add))
                for half in range(2):
                    dve.wait_ge(s_cv, 6 * m + 5 + half)
                    o = yc[:, m, half * 512:(half + 1) * 512]
                    tt(o, o, ps[:, (6 * m + 4 + half) % 4, :], ALU.mult).then_inc(s_y, 1)
                    row_turn(2 + half, half == 0)

            def s5_states(n):
                g = slice(4 * n, 4 * n + 4)
                S4 = ps[:, 4, :].rearrange("p (g c) -> p g c", g=4)
                Ss4 = ps[:, 5, :].rearrange("p (g c) -> p g c", g=4)
                dve.wait_ge(s_s, n + 1)
                if n == 0:
                    dve.wait_ge(s_E, 1)
                    dve.wait_ge(s_Q, 1)
                    step.run(v.memset(R1[:, :, 0:1], 0.0))
                    step.run(v.memset(R2[:, :, 0:1], 0.0))
                step.run(tt(zin[:], S4, cosT[:, g, :], ALU.mult))
                step.run(tt(zt[:], Ss4, sinT[:, g, :], ALU.mult))
                step.settle()
                step(tt(zin[:], zin[:], zt[:], ALU.subtract))
                for gq in range(4):
                    step.run(v.tensor_tensor_scan(zt[:, gq, :], sp[:, 6, 4 * n + gq:4 * n + gq + 1].to_broadcast([P, P]),
                                                  zin[:, gq, :], 0.0, ALU.mult, ALU.add))
                step.settle()
                if n:
                    dve.wait_ge(s_ym, n)
                step(tt(R1[:, :, 1:P + 1], zt[:], cosT[:, g, :], ALU.mult))
                tt(R2[:, :, 1:P + 1], zt[:], sinT[:, g, :], ALU.mult).then_inc(s_r, 1)

            def s5_y(n):
                g = slice(4 * n, 4 * n + 4)
                dve.wait_ge(s_ym, n + 1)
                d = dskip[:, 64 * n:64 * n + 64].rearrange("c (g h) -> c g h", g=4).unsqueeze(2)
                step(tt(zin[:].rearrange("c g (i h) -> c g i h", h=H), U[:, g],
                        d.to_broadcast([P, 4, NT, H]), ALU.mult))
                tt(y[:, g].rearrange("c g i h -> c (g i h)"), zin[:].rearrange("c g s -> c (g s)"), ps[:, 7, :],
                   ALU.add).then_inc(s_ye, 1)

            for m in range(NM):
                first = PER_M * m if m * PER_M < NP else None

                def row_turn(n, then=True):
                    if first is not None:
                        add_row(first + n)
                        if then:
                            partials(first + n + 1)

                if first is not None:
                    partials(first)
                conv_z(m, 0)
                row_turn(0)
                if m == 1:
                    s5_y(0)
                if m == 2:
                    s5_states(2)
                if m == 3:
                    s5_y(3)
                conv_z(m, 1)
                row_turn(1)
                if m == 1:
                    s5_states(1)
                if m == 2:
                    s5_y(2)
                if m == 5:
                    for n in range(4):
                        dve.wait_ge(s_gm, n + 1)
                        tt(glu[:, 2 * n:2 * n + 2, :], ps[:, (4, 5, 7, 6)[n], :].rearrange("c (i d) -> c i d", i=2),
                           bglu[:].unsqueeze(1).to_broadcast([P, 2, D_SSM]), ALU.add).then_inc(s_gb, 1)
                conv(m, row_turn)
                if m == 0:
                    s5_states(0)
                if m == 1:
                    s5_y(1)
                if m == 2:
                    s5_states(3)
                if m == 5:
                    dve.wait_ge(s_gsg, 4)
                    tt(y2[:], y2[:], glu[:], ALU.mult).then_inc(s_y2, 1)
            dve.wait_ge(s_st, 1)
            v.tensor_copy(ss[:, 1, :], ps[:, 6, 0:NT]).then_inc(s_cst, 1)
            dve.wait_ge(s_rmsy, 2)
            step(v.reciprocal(rs[:, 2, :], rs[:, 2, :]))
            step(tt(rs[:, 4, :], rs[:, 1, :], rs[:, 2, :], ALU.mult))
            step(v.reciprocal(rs[:, 1, :], rs[:, 1, :]))
            tt(y2[:], y2[:], rs[:, 4, :].unsqueeze(2).to_broadcast([P, NT, D_SSM]), ALU.mult).then_inc(s_y3, 1)

            dve.wait_ge(s_bc, 64)
            v.scalar_tensor_tensor(scale2[:], scale2[:], 1.0, gffn[:], ALU.add, ALU.mult).then_inc(s_a1, 1)
            dve.wait_ge(s_a1, 2)
            for i in range(NT):
                dve.wait_ge(s_op, i + 1)
                if i >= 2:
                    dve.wait_ge(s_h2st[i % 2], 16 * (i // 2))
                    dve.wait_ge(s_h2t, i - 1)
                b = h2[:, i % 2]
                step(v.scalar_tensor_tensor(b.rearrange("c (n f) -> c n f", n=2),
                                            ps[:, 2 * (i % 2):2 * (i % 2) + 2, :], rs[:, 1, one(i)],
                                            gate1[:].rearrange("c (n f) -> c n f", n=2), ALU.mult, ALU.mult))
                dve.wait_ge(s_x[i], 32)
                tt(x1[:, i], x1[:, i], b, ALU.add).then_inc(s_x1, 1)
                dve.wait_ge(s_rms, NT + i + 1)
                step(v.reciprocal(rs[:, 3, one(i)], rs[:, 3, one(i)]))
                dve.wait_ge(s_x1, i + 1)
                step(v.scalar_tensor_tensor(b, x1[:, i], rs[:, 3, one(i)], scale2[:], ALU.mult, ALU.mult))
                tt(b, b, shift2[:], ALU.add).then_inc(s_h2, 1)

            bc = lambda ap, shape: ap.to_broadcast(shape)
            GS, CG, GB, WS, TOT, NB, PE_, PS_ = range(8)
            small8 = lambda j: rsm[:, j, :].rearrange("c (i g) -> c i g", i=NT)

            def r_groups():
                dve.wait_ge(s_sg, 1)
                dve.wait_ge(s_rc, 2)
                dve.wait_ge(s_small, 16 * 12)
                step(tt(bia[:], sig[:], bc(rb[:].unsqueeze(1), [P, NT, NE]), ALU.add))
                for i in range(NT):
                    for g in range(NGRP):
                        step.run(v.max(m8[:, i, g, :], bia[:, i, g * EPG:(g + 1) * EPG]))
                step.settle()
                step(tt(small8(GS), m8[:, :, :, 0], m8[:, :, :, 1], ALU.add))

            def r_group_choice():
                a_ = bc(small8(GS).unsqueeze(2), [P, NT, NGRP, NGRP])
                b_ = bc(small8(GS).unsqueeze(3), [P, NT, NGRP, NGRP])
                step.run(tt(cmpg[:, 0], a_, b_, ALU.is_gt))
                step.run(tt(cmpg[:, 1], a_, b_, ALU.is_equal))
                step.settle()
                step(tt(cmpg[:, 1], cmpg[:, 1], bc(lowg[:].unsqueeze(1), [P, NT, NGRP, NGRP]), ALU.mult))
                step(tt(cmpg[:, 0], cmpg[:, 0], cmpg[:, 1], ALU.add))
                step(v.tensor_reduce(small8(CG), cmpg[:, 0], AX.X, ALU.add))
                step(ts(small8(CG), small8(CG), float(TOP_G), None, ALU.is_lt))
                step(ts(small8(GB), small8(CG), BIG, -BIG, ALU.mult, ALU.add))
                flat = bia[:].rearrange("c i (g e) -> c i g e", g=NGRP)
                step(tt(flat, flat, bc(small8(CG).unsqueeze(3), [P, NT, NGRP, EPG]), ALU.mult))
                step(tt(flat, flat, bc(small8(GB).unsqueeze(3), [P, NT, NGRP, EPG]), ALU.add))

            def r_top():
                for i in range(NT):
                    step.run(v.max(top8[:, i, :], bia[:, i, :]))
                step.settle()
                for i in range(NT):
                    step.run(v.max_index(topi[:, i, :], top8[:, i, :], bia[:, i, :]))
                step.settle()
                step(v.tensor_copy(top8[:], topi[:]))

            def r_select():
                shape = [P, NT, NE, TOP_K]
                step(tt(eq6[:], bc(iota_e[:].unsqueeze(1).unsqueeze(3), shape),
                        bc(top8[:, :, 0:TOP_K].unsqueeze(2), shape), ALU.is_equal))

            def r_selected():
                step(v.tensor_reduce(sel[:], eq6[:], AX.X, ALU.add))
                v.tensor_copy(selb[:], sel[:]).then_inc(s_sel, 1)

            def r_weights():
                step(tt(rs1[:], sel[:], sig[:], ALU.mult))
                step(v.tensor_reduce(rsm[:, WS, 0:NT], rs1[:], AX.X, ALU.add))
                step(v.reciprocal(rsm[:, WS, NT:2 * NT], rsm[:, WS, 0:NT]))
                step(ts(rsm[:, WS, NT:2 * NT], rsm[:, WS, NT:2 * NT], ROUTED_SCALE, None, ALU.mult))
                step(tt(rs1[:], rs1[:], bc(rsm[:, WS, NT:2 * NT].unsqueeze(2), [P, NT, NE]), ALU.mult))
                step(v.tensor_copy(wparts[:, :, 0, :], rs1[:]))
                step(tt(rs1[:], rs1[:], wparts[:, :, 0, :], ALU.subtract))
                step(v.tensor_copy(wparts[:, :, 1, :], rs1[:]))
                step(tt(rs1[:], rs1[:], wparts[:, :, 1, :], ALU.subtract))
                step(v.tensor_copy(wparts[:, :, 2, :], rs1[:]))

            def r_ranks():
                dve.wait_ge(s_rank, 1)
                v.tensor_copy(dest[:].rearrange("c i e -> c (i e)"), ps[:, 3, :]).then_inc(s_ranke, 1)

            def r_blocks():
                cnt = ps[:, 3, :].rearrange("c (i e) -> c i e", i=NT)
                dve.wait_ge(s_cnt, 1)
                dve.wait_ge(s_ranke, 1)
                step(v.memset(pre[:, 0, :], 0.0))
                for i in range(NT - 1):
                    step(tt(pre[:, i + 1, :], pre[:, i, :], cnt[:, i, :], ALU.add))
                step(tt(rsm[:, TOT, :], pre[:, NT - 1, :], cnt[:, NT - 1, :], ALU.add))
                step.run(tt(dest[:], dest[:], pre[:], ALU.add))
                step(tt(cmp8[:], bc(rsm[:, TOT, :].unsqueeze(2), [P, NE, CAP]),
                        bc(blkb[:, 0:CAP].unsqueeze(1), [P, NE, CAP]), ALU.is_gt))
                step(v.tensor_reduce(rsm[:, NB, :], cmp8[:], AX.X, ALU.add))
                step(ts(rsm[:, NB, :], rsm[:, NB, :], 1.0, None, ALU.max))
                step(v.tensor_tensor_scan(rsm[:, PE_, :], ones[:, 0:1].to_broadcast([P, NE]), rsm[:, NB, :], 0.0,
                                          ALU.mult, ALU.add))
                step(tt(rsm[:, PS_, :], rsm[:, PE_, :], rsm[:, NB, :], ALU.subtract))
                step(ts(rsm[:, PS_, :], rsm[:, PS_, :], float(P), 1.0, ALU.mult, ALU.add))
                step(tt(dest[:], dest[:], bc(rsm[:, PS_, :].unsqueeze(1), [P, NT, NE]), ALU.add))
                step(tt(dest[:], dest[:], sel[:], ALU.mult))
                step(ts(dest[:], dest[:], -1.0, None, ALU.add))
                step(ts(rsm[:, NB, :], rsm[:, PE_, :], part[:, 0:1], None, ALU.is_le))
                step(v.tensor_reduce(eblk[:, 0:1], rsm[:, NB, :], AX.X, ALU.add))
                step(v.tensor_copy(nblk[:], rsm[:, PE_, NE - 1:NE]))
                step(v.tensor_copy(ends[:], rsm[0:1, PE_, :]))
                ts(eblk_i[:], eblk[:, 0:1], float(NE - 1), None, ALU.min).then_inc(s_tab, 1)

            def onehot(i, b):
                e = dve.value_load(blk_row[0:1, bass.ds(i, 1)], min_val=0, max_val=NE - 1)
                v.tensor_copy(wv[b][:, :, 3:6], wparts[:, :, :, bass.ds(e, 1)].rearrange("c i w e -> c i (w e)"))\
                 .then_inc(s_oneh, 1)
                v.scalar_tensor_tensor(oneh[b][:], bc(dest[:, :, bass.ds(e, 1)], [P, NT, P]),
                                       blkb[:, bass.ds(i, 1)], bc(slotn[:].unsqueeze(1), [P, NT, P]),
                                       ALU.subtract, ALU.is_equal).then_inc(s_oneh, 1)

            early = (3, 8)

            def slots(i, b):
                pv = ps[:, 3, 8 * b:8 * b + 6]
                dve.wait_ge(s_prep, i + 1)
                v.tensor_reduce(idt[:, 0:1], pv[:, 0:2], AX.X, ALU.add).then_inc(s_id, 1)
                ts(idt[:, 1:2], pv[:, 2:3], trash[:, 1:2], trash[:, 0:1], ALU.mult, ALU.add).then_inc(s_id, 1)
                v.tensor_reduce(slot_w[b][:], pv[:, 3:6], AX.X, ALU.add).then_inc(s_id, 1)
                dve.wait_ge(s_id, early[i] if isinstance(i, int) and i < 2 else 5 * i + 1)
                tt(slot_id[b][:], idt[:, 0:1], idt[:, 1:2], ALU.add).then_inc(s_slot, 1)

            def hold(i, b):
                v.tensor_copy(held_w[b][:], slot_w[b][:]).then_inc(s_id, 1)
                v.tensor_copy(held_id[b][:], slot_id[b][:]).then_inc(s_id, 1)
                dve.wait_ge(s_id, 5 if isinstance(i, int) and i == 0 else 5 * i + 8)

            def first_slots():
                dve.wait_ge(s_blk, 32)
                dve.wait_ge(s_rc, 3)
                onehot(0, 0)
                onehot(1, 1)
                v.memset(eblk[:, 1:2], 0.0).then_inc(s_route, 1)
                slots(0, 0)

            def second_slots():
                onehot(2, 0)
                dve.wait_ge(s_slot, 1)
                hold(0, 0)
                slots(1, 1)

            portions = {0: [r_groups], 1: [r_group_choice, r_top], 2: [r_select, r_selected],
                        3: [r_ranks, r_weights], 4: [r_blocks], 6: [first_slots], 7: [second_slots]}
            for i in range(NT + 1):
                if i:
                    b = (i - 1) % 2
                    dve.wait_ge(s_ht, i)
                    if i >= 3:
                        dve.wait_ge(s_m2, i - 2)
                    v.tensor_copy(hidT[b][:].rearrange("p k c -> p (k c)"), ps[:, 2, 0:2 * P]).then_inc(s_hte, 1)
                if i < NT:
                    b = i % 2
                    dve.wait_ge(s_sl, i + 1)
                    dve.wait_ge(s_m1, i + 1)
                    if i >= 2:
                        dve.wait_ge(s_ht, i - 1)
                    tt(hid[b][:], sil[b][:], ps[:, b, FE:2 * FE], ALU.mult).then_inc(s_hd, 1)
                for portion in portions.get(i, []):
                    portion()


            def turned_low(i, b):
                for kq in range(2):
                    reached(dve, s_xgA, 2 * i + kq + 1)
                    k4 = slice(4 * kq, 4 * kq + 4)
                    tt(xgl[b][:, k4, :], ps[:, 4 + kq, :].rearrange("p (k c) -> p k c", k=4),
                       xgh[b][:, k4, :].bitcast(F32), ALU.subtract).then_inc(s_xgD, 1)

            def weights_low(e):
                raw = w_raw[:].rearrange("p q a k n -> p (q a k n)")
                for n in range(4):
                    dve.wait_ge(s_whi, e * 4 + n + 1)
                    low = low_of(e) + n * (W13 // 4)
                    tt(w_parts[:, bass.ds(low, W13 // 4)], raw[:, bass.ds(low - W_LO, W13 // 4)],
                       w_parts[:, bass.ds(high_of(e) + n * (W13 // 4), W13 // 4)].bitcast(F32), ALU.subtract)\
                        .then_inc(s_wlo, 1)

            weights_low(0)
            turned_low(0, 0)
            dve.wait_ge(s_xg[0], 16)
            slots(2, 0)
            onehot(3, 1)
            new_expert(dve, 1, weights_low)
            n_blocks = dve.value_load(nblk[0:1, 0:1], min_val=NE, max_val=MAX_BLOCKS)

            def hidden(b):
                v.scalar_tensor_tensor(hid[b][:], sil[b][:], held_w[b][:, 0:1], ps[:, b, FE:2 * FE],
                                       ALU.mult, ALU.mult).then_inc(s_eh, 1)

            def pair(j):
                for i, b in ((2 * j + 1, 1), (2 * j + 2, 0)):
                    reached(dve, s_esl, i)
                    hidden(1 - b)
                    reached(dve, s_sc[1 - b], 16 * j)
                    v.tensor_copy(row_id[1 - b][:], held_id[1 - b][:]).then_inc(s_rid, 1)
                    turned_low(i, b)
                    reached(dve, s_slot, i + 2)
                    hold(i, b)
                    slots(i + 2, b)
                    onehot(i + 3, 1 - b)
                    new_expert(dve, i + 1, weights_low)

            pairs(dve, n_blocks, pair)
            last = (n_blocks // 2) * 2
            dve.wait_ge(s_esl, last + 1)
            hidden(0)
            dve.wait_ge(s_sc[0], 16 * (n_blocks // 2))
            v.tensor_copy(row_id[0][:], held_id[0][:]).then_inc(s_rid, 1)

            dve.wait_ge(s_fbc, 32)
            for i in range(NT + 1):
                if i < NT:
                    f = ffn[:, i]
                    dve.wait_ge(s_x[i], 48)
                    step(tt(f, f, gate2[:], ALU.mult))
                    tt(x1[:, i], x1[:, i], f, ALU.add).then_inc(s_x2, 1)
                if i:
                    dve.wait_ge(s_rms, 2 * NT + i)
                    v.reciprocal(rs[:, 4, one(i - 1)], rs[:, 4, one(i - 1)]).then_inc(s_irms, 1)

        @block.gpsimd
        def _(gp):
            p = nc.gpsimd
            step = Steps(gp, s_gp)
            tt, ts = p.tensor_tensor, p.tensor_scalar
            step(p.memset(ident[:], 0.0))
            step(p.memset(ones[:], 1.0))
            step(p.memset(eps[:], EPS))
            p.affine_select(out=ident[:], in_=ident[:], compare_op=ALU.not_equal, fill=1.0, base=0,
                            pattern=[[-1, P]], channel_multiplier=1).then_inc(s_consts, 1)
            p.memset(T[:], 0.0).then_inc(s_T0, 1)
            gp.wait_ge(s_s5in, 16 * 15)
            step(ts(W0[0:S, 1], W0[0:S, 1], -1.0, None, ALU.mult))
            gp.wait_ge(s_pe, 1)
            gp.wait_ge(s_xt, 16)
            tmp = lambda j: tp[:, j, 0:G * H].rearrange("p (g h) -> p g h", g=G)
            wide = lambda ap: ap.unsqueeze(2).to_broadcast([P, G, H])

            def times(re, im, a, a_s, o, o_s):
                step.run(tt(tmp(0), a, wide(re), ALU.mult))
                step.run(tt(tmp(1), a_s, wide(im), ALU.mult))
                step.run(tt(tmp(2), a_s, wide(re), ALU.mult))
                step.run(tt(tmp(3), a, wide(im), ALU.mult))
                step.settle()
                step.run(tt(o, tmp(0), tmp(1), ALU.add))
                step.run(tt(o_s, tmp(2), tmp(3), ALU.subtract))
                step.settle()

            times(sp[:, 2], sp[:, 3], W0[:, 0], W0[:, 1], V[:, :, NT - 1, :], Vs[:, :, NT - 1, :])
            for m in range(NT - 2, -1, -1):
                times(sp[:, 0], sp[:, 1], V[:, :, m + 1, :], Vs[:, :, m + 1, :], V[:, :, m, :], Vs[:, :, m, :])
            step.settle()
            p.memset(pwt[:, 0, 0:1], 0.0).then_inc(s_V, 1)
            gp.wait_ge(s_adac, 1)
            step.run(p.memset(cosT[:, :, 0:1], 1.0))
            step.run(p.memset(sinT[:, :, 0:1], 0.0))
            step.run(p.tensor_copy(pw[:, 0, :], sp[:, 4, :]))
            step.run(p.tensor_copy(pw[:, 1, :], sp[:, 5, :]))
            step.settle()
            n = 1
            half = lambda j, n: tp[:].rearrange("p a b -> p (a b)")[:, 1024 * j:1024 * j + G * n]\
                .rearrange("p (g c) -> p g c", g=G)
            while n < P:
                wr_ = pw[:, 0, :].unsqueeze(2).to_broadcast([P, G, n])
                wi_ = pw[:, 1, :].unsqueeze(2).to_broadcast([P, G, n])
                step.run(tt(half(0, n), cosT[:, :, 0:n], wr_, ALU.mult))
                step(tt(half(1, n), sinT[:, :, 0:n], wi_, ALU.mult))
                step(tt(cosT[:, :, n:2 * n], half(0, n), half(1, n), ALU.subtract))
                step.run(tt(half(0, n), cosT[:, :, 0:n], wi_, ALU.mult))
                step(tt(half(1, n), sinT[:, :, 0:n], wr_, ALU.mult))
                step(tt(sinT[:, :, n:2 * n], half(0, n), half(1, n), ALU.add))
                step.run(tt(pwt[:, 0, :], pw[:, 1, :], pw[:, 1, :], ALU.mult))
                step(tt(pwt[:, 1, :], pw[:, 0, :], pw[:, 1, :], ALU.mult))
                step.run(ts(pw[:, 0, :], pwt[:, 0, :], -2.0, 1.0, ALU.mult, ALU.add))
                step(ts(pw[:, 1, :], pwt[:, 1, :], 2.0, None, ALU.mult))
                n *= 2
            p.memset(pwt[:, 0, 0:1], 0.0).then_inc(s_E, 1)
            for m in range(NM):
                gp.wait_ge(s_sq, m + 1)
                if m == 0:
                    p.tensor_copy(sqsum[:], sq[:]).then_inc(s_sqs, 1)
                else:
                    gp.wait_ge(s_sqs, m)
                    tt(sqsum[:], sqsum[:], sq[:], ALU.add).then_inc(s_sqs, 1)
            gp.wait_ge(s_op, NT)
            p.memset(zrow[:], 0.0).then_inc(s_zr, 1)
            step.run(p.iota(part[:], [[0, 1]], base=0, channel_multiplier=1, allow_small_or_imprecise_dtypes=True))
            step.run(p.iota(trash[:, 0:1], [[0, 1]], base=SEQ, channel_multiplier=1,
                            allow_small_or_imprecise_dtypes=True))
            step.run(p.iota(slotn[:], [[1, P]], base=0, channel_multiplier=0, allow_small_or_imprecise_dtypes=True))
            step.run(p.iota(blkb[:], [[P, P]], base=0, channel_multiplier=0, allow_small_or_imprecise_dtypes=True))
            step.run(p.iota(iota_e[:], [[1, NE]], base=0, channel_multiplier=0, allow_small_or_imprecise_dtypes=True))
            step.run(p.memset(tri[:], 1.0))
            step.run(p.memset(onesb[:], 1.0))
            step.run(p.memset(lowg[:], 1.0))
            for b in range(2):
                step.run(p.iota(wv[b][:, :, 0], [[0, NT]], base=0, channel_multiplier=NT,
                                allow_small_or_imprecise_dtypes=True))
                step.run(p.iota(wv[b][:, :, 1], [[1, NT]], base=0, channel_multiplier=0,
                                allow_small_or_imprecise_dtypes=True))
                step.run(p.memset(wv[b][:, :, 2], 1.0))
            step.settle()
            step.run(ts(trash[:, 1:2], trash[:, 0:1], -1.0, None, ALU.mult))
            step.run(p.affine_select(out=tri[:], in_=tri[:], compare_op=ALU.is_gt, fill=0.0, base=0,
                                     pattern=[[1, P]], channel_multiplier=-1))
            step.run(p.affine_select(out=lowg[:], in_=lowg[:], compare_op=ALU.is_gt, fill=0.0, base=0,
                                     pattern=[[1, NGRP], [-1, NGRP]], channel_multiplier=0))
            step.settle()
            p.memset(pwt[:, 0, 0:1], 0.0).then_inc(s_rc, 3)

            def gather(b):
                p.indirect_dma_start(out=xg[b][:], out_offset=None, in_=h2_d,
                                     in_offset=bass.IndirectOffsetOnAxis(ap=slot_id[b][:, 0:1], axis=0))\
                 .then_inc(s_xg[b], 16)

            def scatter(b):
                p.indirect_dma_start(out=ffn_d, out_offset=bass.IndirectOffsetOnAxis(ap=row_id[b][:, 0:1], axis=0),
                                     in_=yo[b][:], in_offset=None, compute_op=ALU.add).then_inc(s_sc[b], 16)

            gp.wait_ge(s_h2st[0], 16 * 4)
            gp.wait_ge(s_h2st[1], 16 * 4)
            gp.wait_ge(s_zst, 32)
            gp.wait_ge(s_slot, 1)
            gather(0)
            gp.wait_ge(s_slot, 2)
            gather(1)
            gp.wait_ge(s_syst[0], 16 * 4)
            gp.wait_ge(s_syst[1], 16 * 4)
            n_blocks = gp.value_load(nblk[0:1, 0:1], min_val=NE, max_val=MAX_BLOCKS)

            def settled(n):
                reached(gp, s_tick, n)
                tt(pwt[:, 2, 0:1], pwt[:, 3, 0:1], pwt[:, 3, 0:1], ALU.mult).then_inc(s_tick, 1)

            def pair(j):
                for i, b, ticks in ((2 * j + 1, 1, 4 * j - 1), (2 * j + 2, 0, 4 * j + 1)):
                    first = isinstance(i, int) and i == 1
                    reached(gp, s_slot, i + 2)
                    reached(gp, s_xgt, i)
                    settled(0 if first else ticks)
                    gather(1 - b)
                    if first:
                        continue
                    reached(gp, s_ey, i - 1)
                    reached(gp, s_rid, i - 1)
                    reached(gp, s_sc[1 - b], 16 * j)
                    settled(ticks + 1)
                    scatter(b)

            step(p.memset(pwt[:, 3, 0:1], 0.0))
            pairs(gp, n_blocks, pair)
            last = (n_blocks // 2) * 2
            gp.wait_ge(s_ey, last)
            gp.wait_ge(s_rid, last)
            gp.wait_ge(s_sc[0], 16 * (n_blocks // 2))
            tt(pwt[:, 1, 0:1], pwt[:, 3, 0:1], pwt[:, 3, 0:1], ALU.mult).then_inc(s_tick, 1)
            scatter(1)
            gp.wait_ge(s_ey, last + 1)
            gp.wait_ge(s_rid, last + 1)
            gp.wait_ge(s_sc[1], 16 * (n_blocks // 2))
            settled(2 * last)
            scatter(0)
            gp.wait_ge(s_sc[0], 16 * (n_blocks // 2) + 16)
            gp.wait_ge(s_xg[1], 16 * (n_blocks // 2) + 16)
            settled(2 * last + 1)
            gp.wait_ge(s_zst, 32)
            p.memset(pwt[:, 0, 0:1], 0.0).then_inc(s_fin, 1)
            gp.wait_ge(s_fbc, 32)
            for i in range(NT):
                gp.wait_ge(s_scaled, i + 1)
                tt(res[:, i], res[:, i], gfin[:], ALU.mult).then_inc(s_res, 1)


INPUTS = ["x", "c", "w_ada", "b_ada", "g_mix", "w_in", "conv_w", "conv_b", "g_conv", "lam_re", "lam_im", "log_dt",
          "b_re", "b_im", "c_re", "c_im", "d_skip", "w_glu", "b_glu", "g_ssm", "w_out", "g_ffn", "w_router",
          "router_bias", "w1", "w3", "w2", "ws1", "ws3", "ws2", "g_final"]


def kernel(**inputs):
    import numpy as np
    import concourse.bacc as bacc
    from concourse.bass_utils import run_bass_kernel_spmd

    nc = bacc.Bacc("TRN2", target_bir_lowering=False, num_devices=1)
    arrays, args = {}, []
    for name in INPUTS:
        a = np.ascontiguousarray(inputs[name])
        arrays[f"in_{name}"] = a
        args.append(nc.dram_tensor(f"in_{name}", a.shape, mybir.dt.from_np(a.dtype), kind="ExternalInput").ap())
    out = nc.dram_tensor("out", inputs["x"].shape, F32, kind="ExternalOutput").ap()
    layer_kernel(nc, *args, out)
    r = run_bass_kernel_spmd(nc, [arrays], core_ids=[0])
    return r.results[0]["out"]
```
